# Optimizing a Trainium2 kernel written in Bass

```python
import math
import jax, jax.numpy as jnp
from jax import lax
import numpy as np

D_MODEL = 2048
BATCH = 1
SEQ = 256
DEPTH = 1

GRID_W = 64
CTX_LEN = 256
MIX_W = D_MODEL
LIN_W = MIX_W // 2
POOL_W = MIX_W - LIN_W
N_LIN_HEADS = 8
HEAD_DIM = LIN_W // N_LIN_HEADS
N_DIR = 2
N_POOL_GROUPS = 4
POOL_GROUP_W = POOL_W // N_POOL_GROUPS
POOL_SIZES = (2, 4, 8, 16)
CONV_K = 5
CHUNK = 64
D_FF = 4 * D_MODEL
N_MOD = 6
GATE_START = 3 * LIN_W
DECAY_START = 4 * LIN_W
POOL_START = DECAY_START + 2 * N_DIR * N_LIN_HEADS
IN_COLS = POOL_START + POOL_W
EPS = 1e-6

kernel_name = 'hybrid_deltanet_pool_dit_block'

def rmsnorm(x, w):
    xf = x.astype(jnp.float32)
    y = xf * lax.rsqrt(jnp.mean(xf * xf, axis=-1, keepdims=True) + EPS)
    return y.astype(x.dtype) * w

def l2norm(x):
    xf = x.astype(jnp.float32)
    return (xf * lax.rsqrt(jnp.sum(xf * xf, axis=-1, keepdims=True) + EPS)).astype(x.dtype)

def modulate(xn, shift, scale):
    return xn * (1 + scale) + shift

def short_conv(u, w):
    t = u.shape[1]
    pad = CONV_K // 2
    up = jnp.pad(u, ((0, 0), (pad, pad), (0, 0)))
    out = up[:, 0:t] * w[0]
    for i in range(1, CONV_K):
        out = out + up[:, i:i + t] * w[i]
    return out

def gated_delta_chunked(q, k, v, g, beta, s0):
    b, t, h, dk = k.shape
    dv = v.shape[-1]
    n = t // CHUNK
    f32 = jnp.float32

    def to_chunks(a):
        a = a.astype(f32).reshape((b, n, CHUNK) + a.shape[2:])
        return jnp.moveaxis(a, (1, 2), (0, 3))

    kc, vc, gch, bc = to_chunks(k), to_chunks(v), to_chunks(g), to_chunks(beta)
    gcum = jnp.cumsum(gch, axis=-1)
    incl = jnp.tril(jnp.ones((CHUNK, CHUNK), dtype=bool))
    strict = jnp.tril(jnp.ones((CHUNK, CHUNK), dtype=bool), -1)
    diff = gcum[..., :, None] - gcum[..., None, :]
    decay = jnp.where(incl, jnp.exp(jnp.where(incl, diff, 0.0)), 0.0)
    kb = kc * bc[..., None]
    m = jnp.where(strict, jnp.einsum('nbhid,nbhjd->nbhij', kb, kc) * decay, 0.0)
    tmat = m + jnp.eye(CHUNK, dtype=f32)
    u = lax.linalg.triangular_solve(tmat, vc * bc[..., None], left_side=True, lower=True, unit_diagonal=True)
    w = lax.linalg.triangular_solve(tmat, kb * jnp.exp(gcum)[..., None], left_side=True, lower=True, unit_diagonal=True)
    g_last = gcum[..., -1]
    k_tail = kc * jnp.exp(g_last[..., None] - gcum)[..., None]
    if q is None:
        xs = (u, w, k_tail, g_last, None, None)
    else:
        qc = to_chunks(q)
        intra = jnp.einsum('nbhid,nbhjd->nbhij', qc, kc) * decay
        xs = (u, w, k_tail, g_last, qc * jnp.exp(gcum)[..., None], intra)

    def step(s, inp):
        u_i, w_i, kt_i, gl_i, qd_i, at_i = inp
        v_new = u_i - jnp.einsum('bhck,bhkv->bhcv', w_i, s)
        s_new = s * jnp.exp(gl_i)[..., None, None] + jnp.einsum('bhck,bhcv->bhkv', kt_i, v_new)
        if qd_i is None:
            return s_new, None
        o_i = jnp.einsum('bhck,bhkv->bhcv', qd_i, s) + jnp.einsum('bhij,bhjv->bhiv', at_i, v_new)
        return s_new, o_i

    s_fin, o = lax.scan(step, s0.astype(f32), xs)
    if o is None:
        return None, s_fin
    o = jnp.moveaxis(o, (0, 3), (1, 2)).reshape(b, t, h, dv).astype(v.dtype)
    return o, s_fin

def deltanet_inputs(proj, conv_w, a_log, dt_bias):
    b, t, _ = proj.shape
    qkv = jax.nn.silu(short_conv(proj[..., :GATE_START], conv_w)).reshape(b, t, 3, N_LIN_HEADS, HEAD_DIM)
    q = l2norm(qkv[:, :, 0]) * HEAD_DIM ** -0.5
    k = l2norm(qkv[:, :, 1])
    v = qkv[:, :, 2]
    z = proj[..., GATE_START:DECAY_START].reshape(b, t, N_LIN_HEADS, HEAD_DIM)
    ab = proj[..., DECAY_START:POOL_START].astype(jnp.float32).reshape(b, t, 2, N_DIR, N_LIN_HEADS)
    g = -jnp.exp(a_log.astype(jnp.float32)) * jax.nn.softplus(ab[:, :, 0] + dt_bias.astype(jnp.float32))
    beta = jax.nn.sigmoid(ab[:, :, 1])
    return q, k, v, z, g, beta

def gated_head_norm(o, z, w):
    return (rmsnorm(o, w) * jax.nn.silu(z)).reshape(o.shape[0], o.shape[1], LIN_W)

def flip_t(a):
    return jnp.flip(a, axis=1)

def box_mean(u, size, axis):
    n = u.shape[axis]
    idx = jnp.arange(n)
    lo = jnp.clip(idx - size // 2, 0, n - 1)
    hi = jnp.clip(idx + size - 1 - size // 2, 0, n - 1)
    pad = [(0, 0)] * u.ndim
    pad[axis] = (1, 0)
    csum = jnp.pad(jnp.cumsum(u.astype(jnp.float32), axis=axis), pad)
    total = jnp.take(csum, hi + 1, axis=axis) - jnp.take(csum, lo, axis=axis)
    shape = [1] * u.ndim
    shape[axis] = n
    cnt = (hi - lo + 1).astype(jnp.float32).reshape(shape)
    return (total / cnt).astype(u.dtype)

def pool_mixer(p, pool_w, pool_scale, on_grid):
    b, t, _ = p.shape
    outs = []
    for gi, size in enumerate(POOL_SIZES):
        pg = p[..., gi * POOL_GROUP_W:(gi + 1) * POOL_GROUP_W]
        if on_grid:
            rows = t // GRID_W
            pg2 = pg.reshape(b, rows, GRID_W, POOL_GROUP_W)
            mean = box_mean(box_mean(pg2, size, 1), size, 2).reshape(b, t, POOL_GROUP_W)
        else:
            mean = box_mean(pg, size, 1)
        outs.append((mean - pg) @ pool_w[gi])
    return jnp.concatenate(outs, axis=-1) * pool_scale

def sq_relu_mlp(xn, w_up, w_down):
    return jnp.square(jax.nn.relu(xn @ w_up)) @ w_down

def trunk_layer(x, h, mod, mod_c, norm1_w, norm2_w, w_in, conv_w, a_log, dt_bias, onorm_w,
                pool_w, pool_scale, w_out, w_up, w_down, ctx_out):
    b = x.shape[0]
    xn = modulate(rmsnorm(x, norm1_w), mod[..., 0, :], mod[..., 1, :])
    hn = modulate(rmsnorm(h, norm1_w), mod_c[..., 0, :], mod_c[..., 1, :])
    px = xn @ w_in
    ph = hn @ w_in

    qx, kx, vx, zx, gx, bx = deltanet_inputs(px, conv_w, a_log, dt_bias)
    qh, kh, vh, zh, gh, bh = deltanet_inputs(ph, conv_w, a_log, dt_bias)
    s0 = jnp.zeros((b, N_LIN_HEADS, HEAD_DIM, HEAD_DIM), jnp.float32)
    oh_f, sh_f = gated_delta_chunked(qh if ctx_out else None, kh, vh, gh[:, :, 0], bh[:, :, 0], s0)
    oh_b, sh_b = gated_delta_chunked(flip_t(qh) if ctx_out else None, flip_t(kh), flip_t(vh),
                                     flip_t(gh[:, :, 1]), flip_t(bh[:, :, 1]), s0)
    ox_f, _ = gated_delta_chunked(qx, kx, vx, gx[:, :, 0], bx[:, :, 0], sh_f)
    ox_b, _ = gated_delta_chunked(flip_t(qx), flip_t(kx), flip_t(vx), flip_t(gx[:, :, 1]), flip_t(bx[:, :, 1]), sh_b)
    lin_x = gated_head_norm(ox_f + flip_t(ox_b), zx, onorm_w)

    pool_x = pool_mixer(px[..., POOL_START:], pool_w, pool_scale, True)

    x = x + mod[..., 2, :] * (jnp.concatenate([lin_x, pool_x], axis=-1) @ w_out)
    xn2 = modulate(rmsnorm(x, norm2_w), mod[..., 3, :], mod[..., 4, :])
    x = x + mod[..., 5, :] * sq_relu_mlp(xn2, w_up, w_down)

    if not ctx_out:
        return x, None
    lin_h = gated_head_norm(oh_f + flip_t(oh_b), zh, onorm_w)
    pool_h = pool_mixer(ph[..., POOL_START:], pool_w, pool_scale, False)
    h = h + mod_c[..., 2, :] * (jnp.concatenate([lin_h, pool_h], axis=-1) @ w_out)
    hn2 = modulate(rmsnorm(h, norm2_w), mod_c[..., 3, :], mod_c[..., 4, :])
    h = h + mod_c[..., 5, :] * sq_relu_mlp(hn2, w_up, w_down)
    return x, h

def setup_inputs(seed: int = 0) -> dict:
    key = jax.random.key(seed)
    ks = jax.random.split(key, 20)
    f32 = jnp.float32

    def nrm(k, shape, s):
        return jax.random.normal(k, shape, f32) * s

    x = nrm(ks[0], (BATCH, SEQ, D_MODEL), 1.0)
    c = nrm(ks[1], (BATCH, D_MODEL), 1.0)
    ctx = nrm(ks[2], (BATCH, CTX_LEN, D_MODEL), 1.0)
    c_ctx = nrm(ks[3], (D_MODEL,), 1.0)
    w_ada = nrm(ks[4], (DEPTH, D_MODEL, N_MOD * D_MODEL), 0.5 * D_MODEL ** -0.5)
    b_ada = nrm(ks[5], (DEPTH, N_MOD * D_MODEL), 0.02)
    norm1_w = 1.0 + nrm(ks[6], (DEPTH, D_MODEL), 0.05)
    norm2_w = 1.0 + nrm(ks[7], (DEPTH, D_MODEL), 0.05)
    w_in = nrm(ks[8], (DEPTH, D_MODEL, IN_COLS), D_MODEL ** -0.5)
    conv_w = nrm(ks[9], (DEPTH, CONV_K, 3 * LIN_W), CONV_K ** -0.5)
    a_log = jnp.log(jax.random.uniform(ks[10], (DEPTH, N_DIR, N_LIN_HEADS), f32, 1.0, 16.0))
    dt = jnp.exp(jax.random.uniform(ks[11], (DEPTH, N_DIR, N_LIN_HEADS), f32, math.log(1e-3), math.log(1e-1)))
    dt_bias = dt + jnp.log(-jnp.expm1(-dt))
    onorm_w = 1.0 + nrm(ks[12], (DEPTH, HEAD_DIM), 0.05)
    pool_w = nrm(ks[13], (DEPTH, N_POOL_GROUPS, POOL_GROUP_W, POOL_GROUP_W), POOL_GROUP_W ** -0.5)
    pool_scale = 1.0 + nrm(ks[14], (DEPTH, POOL_W), 0.1)
    w_out = nrm(ks[15], (DEPTH, MIX_W, D_MODEL), MIX_W ** -0.5)
    w_up = nrm(ks[16], (DEPTH, D_MODEL, D_FF), D_MODEL ** -0.5)
    w_down = nrm(ks[17], (DEPTH, D_FF, D_MODEL), D_FF ** -0.5)
    final_norm_w = 1.0 + nrm(ks[18], (D_MODEL,), 0.05)
    return {'x': x, 'c': c, 'ctx': ctx, 'c_ctx': c_ctx, 'w_ada': w_ada, 'b_ada': b_ada,
            'norm1_w': norm1_w, 'norm2_w': norm2_w, 'w_in': w_in, 'conv_w': conv_w,
            'a_log': a_log, 'dt_bias': dt_bias, 'onorm_w': onorm_w, 'pool_w': pool_w,
            'pool_scale': pool_scale, 'w_out': w_out, 'w_up': w_up, 'w_down': w_down,
            'final_norm_w': final_norm_w}

def reference(x, c, ctx, c_ctx, w_ada, b_ada, norm1_w, norm2_w, w_in, conv_w, a_log, dt_bias,
              onorm_w, pool_w, pool_scale, w_out, w_up, w_down, final_norm_w):
    b = x.shape[0]
    sc = jax.nn.silu(c)
    scc = jax.nn.silu(c_ctx)
    h = ctx
    for l in range(DEPTH):
        mod = (sc @ w_ada[l] + b_ada[l]).reshape(b, 1, N_MOD, D_MODEL)
        mod_c = (scc @ w_ada[l] + b_ada[l]).reshape(N_MOD, D_MODEL)
        x, h = trunk_layer(x, h, mod, mod_c, norm1_w[l], norm2_w[l], w_in[l], conv_w[l], a_log[l],
                           dt_bias[l], onorm_w[l], pool_w[l], pool_scale[l], w_out[l], w_up[l],
                           w_down[l], l < DEPTH - 1)
    return rmsnorm(x, final_norm_w)


_drawn_inputs = setup_inputs


def setup_inputs(seed=0):
    import zlib

    import numpy as np

    out = dict(_drawn_inputs(seed))
    spreads = {}
    factors = {'ctx': 4.493,
     'c_ctx': 6.561,
     'norm1_w': 3.699,
     'onorm_w': 8.0,
     'norm2_w': 8.0,
     'pool_scale': 3.443}
    for name, (base, spread) in spreads.items():
        noise = np.random.default_rng([zlib.crc32(name.encode()), seed]).standard_normal(out[name].shape)
        drawn = base * np.exp(spread * noise) if base else spread * noise
        out[name] = __import__('jax').numpy.asarray(drawn.astype(out[name].dtype))
    for name, factor in factors.items():
        out[name] = (out[name] * factor).astype(out[name].dtype)
    return out
```

```python
from contextlib import ExitStack

import concourse.bass as bass
from concourse import mybir
from concourse.bass import ds

F32 = mybir.dt.float32
F32R = mybir.dt.float32r
ALU = mybir.AluOpType
ACT = mybir.ActivationFunctionType

P = 128
D = 2048
KT = D // P
T = 256
NT = 2 * T // P
NH = 8
LIN = 1024
CONV_K = 5
D_FF = 4 * D
FT = D_FF // P
EPS = 1e-6
GRID_W = 64
POOL_SIZES = (2, 4, 8, 16)
DECAY_START = 4 * LIN
POOL_START = DECAY_START + 32
IN_COLS = POOL_START + LIN
NB = 4
BK = KT // NB
UNIT = 2048
HALF = UNIT // 2
NRAW = 4
NHL = 4
CH = P
NCH = NT
NCHAIN = 2 * NH
LEVELS = 6

K_UNITS = [(LIN, 1), (LIN + 512, 1)]
V_UNITS = [(2 * LIN, 1), (2 * LIN + 512, 1)]
Q_UNITS = [(0, 0), (512, 0)]
Z_UNITS = [(3 * LIN, 0), (3 * LIN + 512, 0)]
P_UNITS = [(POOL_START, 0), (POOL_START + 512, 0)]
IN_UNITS = K_UNITS + V_UNITS + Q_UNITS + Z_UNITS + P_UNITS
NU = len(IN_UNITS)
HB = 2 * NU
N_IN = NB * NU
N_OUT = 16
N_UP = 64
N_DOWN = 64


def bank_plan():
    plan, n = [], 0
    for _ in range(NB):
        for _, both in IN_UNITS:
            for _ in range(2):
                plan.append(list(range(n, n + (2 if both else 1))))
                n += len(plan[-1])
    return plan


PLAN = bank_plan()


def build(nc, x, c, ctx_in, c_ctx, w_ada, b_ada, norm1_w, norm2_w, w_in, conv_w, a_log, dt_bias,
          onorm_w, pool_w, pool_scale, w_out, w_up, w_down, final_norm_w, out):
    est = ExitStack()
    with est:
        base = (nc.sbuf_base + 63) // 32 * 32
        limit = nc.sbuf_usable_end
        est.enter_context(nc.allow_non_contiguous_dma(reason="small vectors"))

        def at(name, shape, off, dt=F32):
            size = 4
            for s in shape[1:]:
                size *= s
            assert base + off + size <= limit, (name, off + size, limit - base)
            return nc.alloc_sbuf_tensor_at(name, shape, dt, offset=base + off)

        def sem(name):
            return est.enter_context(nc.semaphore(name))

        KB = 1024
        raw = at("raw", [P, NRAW, UNIT], 0)
        w_hi = at("w_hi", [P, NHL, HALF], 32 * KB, F32R)
        w_lo = at("w_lo", [P, NHL, HALF], 48 * KB, F32R)
        ada = at("ada", [P, 2, UNIT], 64 * KB)
        C0 = 80 * KB
        ident = at("ident", [P, P], C0)
        ones = at("ones", [P, P], C0 + 512)
        col_a = at("col_a", [P, 8, KT], C0 + 1024)
        col_b = at("col_b", [P, P], C0 + 1536)
        cond = at("cond", [P, KT, 2], C0 + 2048)
        scale1 = at("scale1", [P, KT, 2], C0 + 2176)
        shift1 = at("shift1", [P, KT, 2], C0 + 2304)
        scale2 = at("scale2", [P, KT], C0 + 2432)
        shift2 = at("shift2", [P, KT], C0 + 2496)
        ssq = at("ssq", [P, 4], C0 + 2560)
        rms = at("rms", [P, 4], C0 + 2592)
        onorm = at("onorm", [P, 1], C0 + 2624)
        eps_c = at("eps_c", [P, 1], C0 + 2656)
        one_c = at("one_c", [P, 1], C0 + 2688)
        dtb = at("dtb", [P, 16], C0 + 2720)
        alog = at("alog", [P, 16], C0 + 2784)
        gcum = at("gcum", [P, NT, 16], C0 + 2848)
        beta = at("beta", [P, NT, 16], C0 + 3104)
        nbeta = at("nbeta", [P, NT, 16], C0 + 3360)
        neg_eg = at("neg_eg", [P, NT, 16], C0 + 3616)
        e_tail = at("e_tail", [P, NT, 16], C0 + 3872)
        e_last = at("e_last", [P, NT, 16], C0 + 4128)
        R0 = C0 + 4384
        m_low = at("m_low", [P, LEVELS + 1, P], R0)
        m_up = at("m_up", [P, LEVELS + 1, P], R0 + 3584)
        A0 = R0 + 7168
        acc_kv = at("acc_kv", [P, 16, 2 * T], A0)
        acc_x = at("acc_x", [P, 24, T], A0 + 32 * KB)
        F0 = A0 + 56 * KB
        xT = at("xT", [P, KT, 2 * T], F0)
        xn_hi = at("xn_hi", [P, BK, 2 * T], F0 + 32 * KB, F32R)
        xn_lo = at("xn_lo", [P, BK, 2 * T], F0 + 40 * KB, F32R)
        wab_hi = at("wab_hi", [P, KT, 32], F0 + 48 * KB, F32R)
        wab_lo = at("wab_lo", [P, KT, 32], F0 + 50 * KB, F32R)
        ada_acc = at("ada_acc", [P, UNIT], F0 + 52 * KB)
        x_nat = at("x_nat", [P, NT, D], A0)
        wab_raw = at("wab_raw", [P, KT, 32], A0 + 32 * KB)
        rows_a = at("rows_a", [P, P], A0 + 34 * KB)
        rows_b = at("rows_b", [P, P], A0 + 34 * KB + 512)
        XT = at("XT", [P, NCHAIN, 512], F0)
        At = at("At", [P, NCHAIN, T], F0 + 32 * KB)
        KK = at("KK", [P, 2, 512], F0 + 48 * KB)
        QK = at("QK", [P, 2, T], F0 + 52 * KB)
        gcT = at("gcT", [16, 512], F0 + 54 * KB)
        Eb = at("Eb", [P, 2, 512], F0 + 56 * KB)
        Xb = at("Xb", [P, 2, 4, 512], 32 * KB)
        MT = at("MT", [P, 2, 4, 512], 48 * KB)
        sel = at("sel", [16, 16, P], 64 * KB)
        Mn = at("Mn", [P, 512], 72 * KB)
        Pb = at("Pb", [P, 2, 512], 74 * KB)
        tri = at("tri", [P, 4, P], 78 * KB)
        UI, LI, SU, SL = range(4)
        cbuf = at("cbuf", [P, 2, 512], 32 * KB)
        sqb = at("sqb", [P, 2, 512], 36 * KB)
        rsb = at("rsb", [P, 2, 512], 40 * KB)
        lnb = at("lnb", [P, 512], 44 * KB)
        g_in = at("g_in", [P, NT, 16], 46 * KB)
        g_t1 = at("g_t1", [P, NT, 16], 46 * KB + 256)
        g_t2 = at("g_t2", [P, NT, 16], 46 * KB + 512)
        g_log = at("g_log", [P, NT, 16], 46 * KB + 768)
        k_nat = at("k_nat", [P, NH, NCH, P], 32 * KB)
        qd_b = at("qd_b", [P, NH, T], 48 * KB)
        rb = at("rb", [P, 4, 512], 56 * KB)
        vn = at("vn", [P, 4, 512], 64 * KB)
        vt = at("vt", [P, 4, 512], 72 * KB)
        Sb = at("Sb", [P, NCHAIN, P], F0 + 48 * KB)
        eg_row = at("eg_row", [P, 2, T], F0 + 56 * KB)
        pp = at("pp", [P, 2, 8, 80], R0)
        icol = at("icol", [P, 4, GRID_W], R0 + 5120)
        inv = at("inv", [P, 4, GRID_W], R0 + 6144)
        o_sb = at("o_sb", [P, NH, T], 32 * KB)
        o_sq = at("o_sq", [P, NH, T], 40 * KB)
        o_rs = at("o_rs", [P, NH, T], 48 * KB)
        mixT = at("mixT", [P, KT, T], A0)
        mix_hi = at("mix_hi", [P, KT, T], F0, F32R)
        mix_lo = at("mix_lo", [P, KT, T], F0 + 16 * KB, F32R)
        g1_acc = at("g1_acc", [P, UNIT], F0 + 32 * KB)
        gate1 = at("gate1", [P, D], F0 + 40 * KB)
        yt = at("yt", [P, 2, 512], F0 + 48 * KB)
        x2 = at("x2", [P, 2, D], R0 + 24 * KB + 64 * KB + 32 * KB - 120 * KB)
        g2_acc = at("g2_acc", [P, UNIT], R0 + 16 * KB)
        xn2_hi = at("xn2_hi", [P, KT, T], R0 + 24 * KB, F32R)
        xn2_lo = at("xn2_lo", [P, KT, T], R0 + 40 * KB, F32R)
        hT = at("hT", [P, FT, T], R0 + 56 * KB)
        xs2 = at("xs2", [P, 2, D], R0 + 56 * KB)
        xT2 = at("xT2", [P, KT, T], R0 + 72 * KB)
        sq2 = at("sq2", [P, 2, D], R0 + 88 * KB)
        gate2 = at("gate2", [P, D], R0 + 24 * KB)
        fin_w = at("fin_w", [P, D], R0 + 32 * KB)
        h_hi = at("h_hi", [P, 4, T], R0 + 40 * KB, F32R)
        h_lo = at("h_lo", [P, 4, T], R0 + 44 * KB, F32R)
        zero_r = at("zero_r", [P, 512], R0 + 48 * KB, F32R)
        yt2 = at("yt2", [P, 2, 512], R0 + 50 * KB)

        ps = est.enter_context(nc.psum_tensor("ps", [P, 8, 512], F32))

        S = {}

        def s(name):
            if name not in S:
                S[name] = sem(name)
            return S[name]

        raw_in = [sem(f"raw_in{i}") for i in range(NRAW)]
        ada_in = [sem(f"ada_in{i}") for i in range(2)]
        gate_in = [sem(f"gate_in{i}") for i in range(2)]
        x_in = [sem(f"x_in{i}") for i in range(NT)]
        block = est.enter_context(nc.Block())
        w_ada0, w_in0, w_out0, w_up0, w_down0 = w_ada[0], w_in[0], w_out[0], w_up[0], w_down[0]

        def unit_src(n):
            if n < N_IN:
                b, u = n // NU, n % NU
                c0 = IN_UNITS[u][0]
                return w_in0[b * 512:(b + 1) * 512, c0:c0 + 512].rearrange("(k p) c -> p k c", p=P)
            if n < N_IN + N_OUT:
                m = n - N_IN
                ch, k2 = m // 8, m % 8
                return w_out0[k2 * 256:(k2 + 1) * 256, ch * 1024:(ch + 1) * 1024].rearrange("(k p) c -> p k c", p=P)
            raise AssertionError

        def unit_dst(slot, form):
            k = 4 if form == 4 else 2
            return raw[:, slot, :].rearrange("p (k c) -> p k c", k=k)

        def load_unit(eng, n):
            if n >= NRAW:
                eng.wait_ge(s("lo_done"), 2 * (n - NRAW) + 2)
            eng.dma_start(unit_dst(n % NRAW, 4 if n < N_IN else 2), unit_src(n)).then_inc(raw_in[n % NRAW], 16)

        def raw_half(n2, strided):
            slot, hb = (n2 // 2) % NRAW, n2 % 2
            if strided:
                return raw[:, slot, :].rearrange("p (k c) -> p k c", k=4)[:, :, hb * 256:(hb + 1) * 256]
            return raw[:, slot, hb * HALF:(hb + 1) * HALF]

        def part_slot(t, n2, strided):
            v = t[:, n2 % NHL, :]
            return v.rearrange("p (k c) -> p k c", k=4) if strided else v

        def hi_split(eng, n2):
            strided = n2 < 2 * N_IN
            if n2 % 2 == 0:
                eng.wait_ge(raw_in[(n2 // 2) % NRAW], 16 * (n2 // 2 // NRAW + 1))
            if n2 >= NHL:
                wait_used(eng, n2 - NHL)
            eng.activation(part_slot(w_hi, n2, strided), raw_half(n2, strided), ACT.Copy).then_inc(s("hi_done"), 1)

        def lo_split(eng, n2):
            strided = n2 < 2 * N_IN
            eng.wait_ge(s("hi_done"), n2 + 1)
            eng.tensor_tensor(part_slot(w_lo, n2, strided), raw_half(n2, strided),
                              part_slot(w_hi, n2, strided).bitcast(F32), ALU.subtract).then_inc(s("lo_done"), 1)

        ada_stream = [("mod", 0, j) for j in range(8)]
        for b in range(NB):
            for j in range(8):
                ada_stream.append(("row", b, j))
                if b < NB - 1:
                    ada_stream.append(("mod", b + 1, j))
        ada_slot, ada_count, seen = {}, {}, [0, 0]
        last_use = [None, None]
        ada_wait = {}
        for i, it in enumerate(ada_stream):
            sl = (1 if it[0] == "mod" else 0) if i >= 8 else i % 2
            ada_slot[it] = sl
            seen[sl] += 1
            ada_count[it] = seen[sl]
            ada_wait[it] = last_use[sl]
            last_use[sl] = it

        def mod_no(b, j):
            return 8 * b + j + 1

        def row_no(b, j):
            return 8 * b + j + 1

        def load_ada(eng, it):
            prev = ada_wait[it]
            if prev is not None:
                if prev[0] == "mod":
                    eng.wait_ge(s("ada_pe"), mod_no(*prev[1:]))
                else:
                    eng.wait_ge(s("ada_dve"), row_no(*prev[1:]))
            kind, b, j = it
            if kind == "mod":
                part, g = j // 4, j % 4
                src = w_ada0[g * 512:(g + 1) * 512, part * D + b * 512:part * D + (b + 1) * 512]
                eng.dma_start(ada[:, ada_slot[it], :].rearrange("p (k c) -> p k c", k=4),
                              src.rearrange("(k p) c -> p k c", p=P)).then_inc(ada_in[ada_slot[it]], 16)
            else:
                part, kk = 3 + b // 2, 8 * (b % 2) + j
                eng.dma_start(ada[:, ada_slot[it], :],
                              w_ada0[kk * P:(kk + 1) * P, part * D:(part + 1) * D]).then_inc(ada_in[ada_slot[it]], 16)

        def wait_used(eng, n2):
            if n2 < 2 * N_IN:
                eng.wait_ge(s("pj"), PLAN[n2][-1] + 1)
            else:
                eng.wait_ge(s("w_used"), n2 - 2 * N_IN + 1)

        N_MASKS = 2 + (LEVELS + 1) * 6 + 2 + 5
        N0 = PLAN[HB - 1][-1] + 1
        PJ_DVE = PLAN[-1][-1] + 1 - N0

        def tap(i, k):
            tile = (i + 8) if i < 16 else i - 16
            return col_b[:, k * 24 + tile:k * 24 + tile + 1]

        def gb_bank(r):
            return 6 + r % 2

        def t1_bank(r):
            return 7 - r % 2

        def t2_bank(r):
            return 6 + r % 2

        def inverted(r):
            return 24 * (r // 4) + 20 + r % 4 + 1

        def chunk_at(st, d):
            return ((2, 3, 0, 1), (3, 2, 1, 0))[d][st]

        def bc(ap, n):
            return ap.unsqueeze(1).to_broadcast([P, n, ap.shape[-1]])

        def bc_in(ap, n):
            return ap.unsqueeze(2).to_broadcast([P, ap.shape[-1], n])

        def acc_of(u, hb, i, both):
            if both:
                return acc_kv[:, 4 * u + 2 * hb + i, :]
            t = 4 * (u - 4) + 2 * hb
            return acc_x[:, t:t + 2, :].rearrange("p a c -> p (a c)")

        @block.sync
        def _(sp):
            for t in range(NT):
                src = (x if t < 2 else ctx_in)[0][(t % 2) * P:(t % 2 + 1) * P, :]
                sp.dma_start(x_nat[:, t, :], src).then_inc(x_in[t], 16)
            for n in range(NRAW):
                load_unit(sp, n)
            for n in range(NRAW, N_IN):
                load_unit(sp, n)
            for n in range(N_IN, N_IN + NRAW):
                load_unit(sp, n)
            sp.wait_ge(s("o_mm"), 1)
            sp.dma_start(ada[:, 1, :].rearrange("p (k c) -> p k c", k=8),
                         pool_w[0].rearrange("g (i p) o -> p (g i) o", p=P)).then_inc(gate_in[1], 16)
            sp.wait_ge(s("g1_z"), 1)
            sp.dma_start(g1_acc[0:1, :], b_ada[0:1, 2 * D:3 * D]).then_inc(s("g1_b"), 16)
            n_out = N_IN + NRAW
            for kk in range(KT):
                if kk == 1:
                    sp.wait_ge(s("pw_mm"), 8)
                elif kk >= 2:
                    sp.wait_ge(s("ada_dve"), 32 + kk - 1)
                sp.dma_start(ada[:, kk % 2, :], w_ada0[kk * P:(kk + 1) * P, 2 * D:3 * D]).then_inc(gate_in[kk % 2], 16)
                if kk == 3:
                    sp.wait_ge(s("mixl"), KT)
                    sp.dma_start(x2[:, :, :], x[0].rearrange("(t p) d -> p t d", p=P)).then_inc(s("xres_in"), 16)
                if kk >= 2 and kk % 2 == 0:
                    load_unit(sp, n_out)
                    n_out += 1
            for n in range(n_out, N_IN + N_OUT):
                load_unit(sp, n)
            U0 = N_IN + N_OUT

            def up_unit(it, k):
                sp.wait_ge(s("lo_done"), it * 16 + 2 * (U0 + k - NRAW) + 2)
                sp.dma_start(unit_dst(k % NRAW, 4),
                             w_up0[(k % 4) * 512:(k % 4 + 1) * 512, ds(it * 1024 + (k // 4) * 512, 512)]
                             .rearrange("(k p) c -> p k c", p=P)).then_inc(raw_in[k % NRAW], 16)

            def gate_unit(it, j):
                sp.wait_ge(s("ada_dve"), it * 2 + 48 + j - 1)
                sp.dma_start(ada[:, j, :], w_ada0[ds(it * (2 * P) + j * P, P), 5 * D:6 * D]).then_inc(gate_in[j], 16)

            sp.wait_ge(s("g2_z"), 1)
            sp.dma_start(g2_acc[0:1, :], b_ada[0:1, 5 * D:6 * D]).then_inc(s("g2_b"), 16)
            with sp.Fori(0, 8) as it:
                for k in range(8):
                    up_unit(it, k)
                    if k in (2, 6):
                        gate_unit(it, k // 4)
            D0 = U0 + N_UP
            sp.wait_ge(s("w_used"), 2 * (N_OUT + N_UP))
            sp.dma_start(fin_w[:, :], final_norm_w.partition_broadcast(P)).then_inc(s("fin_in"), 16)
            for ch in range(2):
                with sp.Fori(0, 8) as it:
                    for k in range(4):
                        sp.wait_ge(s("lo_done"), it * 8 + 2 * (D0 + 32 * ch + k - NRAW) + 2)
                        sp.dma_start(unit_dst(k % NRAW, 2),
                                     w_down0[ds(it * 1024 + k * 256, 256), ch * 1024:(ch + 1) * 1024]
                                     .rearrange("(k p) c -> p k c", p=P)).then_inc(raw_in[k % NRAW], 16)
            for t in range(2):
                sp.wait_ge(s("fin_c"), t + 1)
                sp.dma_start(out[0][t * P:(t + 1) * P, :], x2[:, t, :]).then_inc(s("stored"), 16)
            sp.wait_ge(s("stored"), 32)

        @block.gpsimd
        def _(pool):
            pool.memset(ones[:, :], 1.0).then_inc(s("const_z"), 1)
            pool.memset(ident[:, :], 0.0).then_inc(s("const_z"), 1)
            pool.memset(eps_c[:, :], EPS).then_inc(s("const_z"), 1)
            pool.memset(one_c[:, :], 1.0).then_inc(s("const_z"), 1)
            pool.wait_ge(s("const_z"), 4)
            pool.affine_select(out=ident[:, :], in_=ident[:, :], compare_op=ALU.not_equal, fill=1.0, base=0,
                               pattern=[[-1, P]], channel_multiplier=1).then_inc(s("const_done"), 1)
            for it in ada_stream[:8]:
                load_ada(pool, it)
            pool.memset(m_low[:, :, :], 0.0).then_inc(s("masks"), 1)
            pool.memset(m_up[:, :, :], 0.0).then_inc(s("masks"), 1)
            pool.wait_ge(s("masks"), 2)
            n = 2
            for lv in range(LEVELS + 1):
                hw, nb = 1 << lv, P >> (lv + 1)
                lo_v = m_low[:, lv, :].rearrange("p (b t j) -> p b t j", t=2, j=hw)
                up_v = m_up[:, lv, :].rearrange("p (b t j) -> p b t j", t=2, j=hw)
                pool.memset(lo_v[:, :, 0, :], 1.0).then_inc(s("masks"), 1)
                pool.memset(up_v[:, :, 1, :], 1.0).then_inc(s("masks"), 1)
                n += 2
                pool.wait_ge(s("masks"), n)
                for v, base_ge, base_le in ((m_low, -hw, 2 * hw - 1), (m_up, 0, hw - 1)):
                    w = v[:, lv, :].rearrange("p (b j) -> p b j", j=2 * hw)
                    pool.affine_select(out=w, in_=w, compare_op=ALU.is_ge, fill=0.0, base=base_ge,
                                       pattern=[[-2 * hw, nb], [0, 2 * hw]], channel_multiplier=1
                                       ).then_inc(s("masks"), 1)
                    n += 1
                    pool.wait_ge(s("masks"), n)
                    pool.affine_select(out=w, in_=w, compare_op=ALU.is_ge, fill=0.0, base=base_le,
                                       pattern=[[2 * hw, nb], [0, 2 * hw]], channel_multiplier=-1
                                       ).then_inc(s("masks"), 1)
                    n += 1
            for it in ada_stream[8:]:
                load_ada(pool, it)
            pool.wait_ge(s("ada_dve"), 32)
            pool.wait_ge(s("ada_pe"), 32)
            pool.memset(tri[:, :, :], 1.0).then_inc(s("masks"), 1)
            pool.memset(sel[:, :, :], 0.0).then_inc(s("masks"), 1)
            n += 2
            pool.wait_ge(s("masks"), n)
            for i, (sgn, b0) in enumerate([(1, 0), (-1, 0), (1, -1), (-1, -1)]):
                pool.affine_select(out=tri[:, i, :], in_=tri[:, i, :], compare_op=ALU.is_ge, fill=0.0, base=b0,
                                   pattern=[[sgn, P]], channel_multiplier=-sgn).then_inc(s("masks"), 1)
                n += 1
            pool.affine_select(out=sel[:, :, :], in_=sel[:, :, :], compare_op=ALU.not_equal, fill=1.0, base=0,
                               pattern=[[-1, 16], [0, P]], channel_multiplier=1).then_inc(s("masks"), 1)
            n += 1
            assert n == N_MASKS, n
            for r in range(NCHAIN):
                h, d = r // 2, r % 2
                pool.wait_ge(s("kk_ev"), 4 * (h + 1))
                pool.wait_ge(s("e_exp"), r + 1)
                pool.tensor_tensor(At[:, r, :], QK[:, d, :], Eb[:, r % 2, 0:T], ALU.mult).then_inc(s("at_pool"), 1)
                pool.wait_ge(s("at_pool"), r + 1)
                pool.tensor_tensor(Eb[:, r % 2, :], KK[:, d, :], Eb[:, r % 2, :], ALU.mult).then_inc(s("am_pool"), 1)
            pool.wait_ge(s("x_upd"), inverted(NCHAIN - 1))
            n = 0

            def step(ins):
                nonlocal n
                n += 1
                ins.then_inc(s("pcnt"), 1)
                pool.wait_ge(s("pcnt"), n)

            step(pool.memset(pp[:, :, :, :], 0.0))
            HWP = 8
            for g, size in enumerate(POOL_SIZES):
                def count(i, nn):
                    return min(i + size - 1 - size // 2, nn - 1) - max(i - size // 2, 0) + 1
                counts = [count(i, GRID_W) for i in range(GRID_W)]
                step(pool.memset(icol[:, g, :], 1.0 / size))
                i = 0
                while i < GRID_W:
                    if counts[i] != size:
                        step(pool.memset(icol[:, g, i:i + 1], 1.0 / counts[i]))
                    i += 1
                for rr in range(4):
                    step(pool.tensor_scalar(inv[:, rr, :], icol[:, g, :], 1.0 / count(rr, 4), None, ALU.mult))
                u = acc_x[:, 16 + 2 * g:18 + 2 * g, :].rearrange("p a (r c) -> p (a r) c", c=GRID_W)
                cur = 0
                step(pool.tensor_copy(pp[:, 0, :, HWP:HWP + GRID_W], u))
                if g:
                    step(pool.memset(pp[:, 0, :, 0:HWP], 0.0))
                    step(pool.memset(pp[:, 0, :, HWP + GRID_W:], 0.0))
                w = 1
                while w < size:
                    lo_s, hi_s = (1, 0) if w == 1 else (w // 2, w // 2)
                    a, bnd = lo_s, 80 - hi_s
                    src, dst = pp[:, cur], pp[:, 1 - cur]
                    if a:
                        step(pool.memset(dst[:, :, 0:a], 0.0))
                    if bnd < 80:
                        step(pool.memset(dst[:, :, bnd:80], 0.0))
                    step(pool.tensor_tensor(dst[:, :, a:bnd], src[:, :, a - lo_s:bnd - lo_s],
                                            src[:, :, a + hi_s:bnd + hi_s], ALU.add))
                    cur, w = 1 - cur, 2 * w
                src = pp[:, cur, :, HWP:HWP + GRID_W].rearrange("p (a r) c -> p a r c", r=4)
                dst = pp[:, 1 - cur, :, HWP:HWP + GRID_W].rearrange("p (a r) c -> p a r c", r=4)
                lo_w, hi_w = size // 2, size - 1 - size // 2
                for rr in range(4):
                    lo_r, hi_r = max(rr - lo_w, 0), min(rr + hi_w, 3)
                    step(pool.tensor_copy(dst[:, :, rr, :], src[:, :, lo_r, :]))
                    for r2 in range(lo_r + 1, hi_r + 1):
                        step(pool.tensor_tensor(dst[:, :, rr, :], dst[:, :, rr, :], src[:, :, r2, :], ALU.add))
                for a_ in range(2):
                    step(pool.tensor_tensor(dst[:, a_], dst[:, a_], inv[:, :, :], ALU.mult))
                pool.tensor_tensor(u, pp[:, 1 - cur, :, HWP:HWP + GRID_W], u, ALU.subtract).then_inc(s("pool_d"), 1)
                pool.wait_ge(s("pool_d"), g + 1)
            pool.wait_ge(s("o_mm"), 1)
            pool.memset(g1_acc[:, :], 0.0).then_inc(s("g1_z"), 1)
            pool.wait_ge(s("mixl"), KT)
            pool.memset(g2_acc[:, :], 0.0).then_inc(s("g2_z"), 1)
            pool.wait_ge(s("w_used"), 2 * (N_OUT + N_UP))
            pool.memset(zero_r[:, :].bitcast(F32), 0.0).then_inc(s("zr"), 1)

        @block.scalar
        def _(act):
            sm = s("rows_in")
            vecs = [c, c_ctx.rearrange("(a d) -> a d", a=1), norm1_w, norm2_w] + \
                   [b_ada[0:1, p * D:(p + 1) * D] for p in (0, 1, 3, 4)]
            for i, v in enumerate(vecs):
                act.dma_start(rows_a[KT * i:KT * (i + 1), :], v[0].rearrange("(k p) -> k p", p=P)).then_inc(sm, 16)
            act.dma_start(rows_b[0:120, :], conv_w[0].rearrange("k (j p) -> (k j) p", p=P)).then_inc(sm, 16)
            act.dma_start(rows_b[120:128, :], pool_scale[0].rearrange("(j p) -> j p", p=P)).then_inc(sm, 16)
            sm = s("small_in")
            act.dma_start(wab_raw[:, :, :],
                          w_in0[:, DECAY_START:POOL_START].rearrange("(k p) c -> p k c", p=P)).then_inc(sm, 16)
            act.dma_start(dtb[:, :], dt_bias[0].rearrange("a b -> (a b)").partition_broadcast(P)).then_inc(sm, 16)
            act.dma_start(alog[:, :], a_log[0].rearrange("a b -> (a b)").partition_broadcast(P)).then_inc(sm, 16)
            act.dma_start(onorm[:, :], onorm_w[0].rearrange("(p o) -> p o", o=1)).then_inc(sm, 16)
            act.wait_ge(s("cols_dve"), 1)
            act.activation(cond[:, :, :], col_a[:, 0:2, :].rearrange("p j k -> p k j"), ACT.Silu
                           ).then_inc(s("cond_done"), 1)
            act.wait_ge(s("small_in"), 64)
            act.activation(wab_hi[:, :, :], wab_raw[:, :, :], ACT.Copy).then_inc(s("wab_h"), 1)
            for t in range(NT):
                act.wait_ge(x_in[t], 16)
                if t:
                    act.wait_ge(s("sq_done"), t)
                act.activation(xT[:, 0:4, :].rearrange("p k c -> p (k c)"), x_nat[:, t, :], ACT.Square,
                               accum_out=ssq[:, t:t + 1]).then_inc(s("sq_done"), 1)
            act.wait_ge(s("sq_done"), NT)
            act.wait_ge(s("const_z"), 4)
            act.activation(rms[:, :], ssq[:, :], ACT.Ln, bias=eps_c[:, :], scale=1.0 / D).then_inc(s("ms"), 1)
            act.wait_ge(s("ms"), 1)
            act.activation(rms[:, :], rms[:, :], ACT.Exp, scale=-0.5).then_inc(s("rms_done"), 1)
            for n2 in range(3):
                hi_split(act, n2)
            for kt in range(0, KT, 2):
                act.wait_ge(s("xt_mm"), kt + 1)
                act.copy(xT[:, kt, :], ps[:, kt % 4, :]).then_inc(s("xt_act"), 1)

            def evac_in(m):
                both, u, hb = IN_UNITS[m // 2 % NU][1], m // 2 % NU, m % 2
                for i, no in enumerate(PLAN[m]):
                    act.wait_ge(s("pj"), no + 1)
                    act.copy(acc_of(u, hb, i, both), ps[:, no % 4, :]).then_inc(s("pj_act"), 1)

            for b in range(NB):
                for m in range(HB):
                    n2 = HB * b + m
                    if n2 >= 3:
                        hi_split(act, n2)
                        if n2 - 3 < HB:
                            evac_in(n2 - 3)
                    if m == 2:
                        for kt in range(BK):
                            if b and kt == 0:
                                wait_used(act, HB * b - 1)
                            act.wait_ge(s("mod_done"), 4 * b + kt + 1)
                            act.copy(xn_hi[:, kt, :], xT[:, BK * b + kt, :]).then_inc(s("xnh"), 1)
            wait_used(act, 2 * N_IN - 1)

            def conv_in(i):
                return acc_kv[:, i, :] if i < 16 else acc_x[:, i - 16, :]

            def centre(i):
                n = 512 if i < 16 else 256
                act.wait_ge(s("pj_dve"), PJ_DVE)
                if i >= 2:
                    act.wait_ge(s("silu"), i - 1)
                act.activation(cbuf[:, i % 2, 0:n], conv_in(i), ACT.Copy, scale=tap(i, 2)).then_inc(s("conv0"), 1)

            centre(0)
            for i in range(24):
                if i + 1 < 24:
                    centre(i + 1)
                n = 512 if i < 16 else 256
                act.wait_ge(s("conv"), 4 * (i + 1))
                act.activation(conv_in(i), cbuf[:, i % 2, 0:n], ACT.Silu).then_inc(s("silu"), 1)
            act.activation(acc_x[:, 8:16, :], acc_x[:, 8:16, :], ACT.Silu).then_inc(s("zsilu"), 1)
            act.wait_ge(s("gp"), 3)
            act.activation(g_t2[:, :, :], g_t1[:, :, :], ACT.Exp).then_inc(s("gp_act"), 1)
            act.activation(beta[:, :, :], nbeta[:, :, :], ACT.Exp, scale=-1.0).then_inc(s("gp_act"), 1)
            act.wait_ge(s("gp_act"), 2)
            act.activation(alog[:, :], alog[:, :], ACT.Exp).then_inc(s("gp_act"), 1)
            act.activation(g_t2[:, :, :], g_t2[:, :, :], ACT.Ln, bias=one_c[:, :]).then_inc(s("gp_act"), 1)
            def l2_src(j):
                return acc_kv[:, j, :] if j < 8 else acc_x[:, 2 * (j - 8):2 * (j - 8) + 2, :].rearrange("p a c -> p (a c)")

            def l2_square(j):
                act.wait_ge(s("silu"), 24)
                if j >= 2:
                    act.wait_ge(s("l2_mm"), j - 1)
                act.activation(sqb[:, j % 2, :], l2_src(j), ACT.Square).then_inc(s("l2_sq"), 1)

            l2_square(0)
            for j in range(12):
                if j + 1 < 12:
                    l2_square(j + 1)
                act.wait_ge(s("l2_mm"), j + 1)
                if j:
                    act.wait_ge(s("l2_rs"), 2 * j)
                act.activation(lnb[:, :], ps[:, j % 2, :], ACT.Ln, bias=eps_c[:, :]).then_inc(s("l2_rs"), 1)
                act.wait_ge(s("l2_rs"), 2 * j + 1)
                if j >= 2:
                    act.wait_ge(s("l2_done"), j - 1)
                act.activation(rsb[:, j % 2, :], lnb[:, :], ACT.Exp, scale=-0.5).then_inc(s("l2_rs"), 1)
            act.wait_ge(s("gc_ev"), 3)
            act.activation(neg_eg[:, :, :], gcum[:, :, :], ACT.Exp).then_inc(s("gp_act"), 1)
            act.activation(e_tail[:, :, :], e_tail[:, :, :], ACT.Exp).then_inc(s("gp_act"), 1)
            act.activation(e_last[:, :, :], e_last[:, :, :], ACT.Exp).then_inc(s("gp_act"), 1)
            act.wait_ge(s("gcT_mm"), 1)
            act.copy(gcT[:, :], ps[0:16, 5, :]).then_inc(s("gcT_ev"), 1)
            for r in range(NCHAIN):
                act.wait_ge(s("gb_ev"), 4 * (r + 1))
                act.activation(Eb[:, r % 2, :], Eb[:, r % 2, :], ACT.Exp).then_inc(s("e_exp"), 1)
                act.wait_ge(s("t2_mm"), r + 1)
                if r >= 8:
                    act.wait_ge(s("x_upd"), inverted(r - 8 + 3 - r % 4))
                act.copy(MT[:, (r // 4) % 2, r % 4, :], ps[:, t2_bank(r), :]).then_inc(s("mt_ev"), 1)
            for r in range(NCHAIN):
                act.wait_ge(s("er_mm"), r + 1)
                if r >= 2:
                    act.wait_ge(s("qd"), r - 1)
                act.activation(eg_row[:, r % 2, :], ps[:, r % 2, 0:T], ACT.Exp).then_inc(s("er_exp"), 1)
                if r < NH:
                    act.wait_ge(s("x_upd"), inverted(NCHAIN - 1))
                    act.wait_ge(s("ktr"), r + 1)
                    act.copy(k_nat[:, r].rearrange("p a b -> p (a b)"), ps[:, 2 + r % 2, :]).then_inc(s("kn_ev"), 1)
            for st in range(3):
                for g in range(4):
                    act.wait_ge(s("vn_ev"), 4 * st + g + 1)
                    if st:
                        act.wait_ge(s("su_mm"), 4 * (st - 1) + g + 1)
                    for q in range(4):
                        h, d = 2 * g + q // 2, q % 2
                        t = chunk_at(st, d)
                        act.activation(vt[:, g, q * P:(q + 1) * P], vn[:, g, q * P:(q + 1) * P], ACT.Copy,
                                       scale=e_tail[:, t, 8 * d + h:8 * d + h + 1]).then_inc(s("vt_ev"), 1)
            act.wait_ge(s("o_ev"), 4)
            act.activation(o_sq[:, :, :], o_sb[:, :, :], ACT.Square).then_inc(s("o_sqd"), 1)
            for i in range(4):
                act.wait_ge(s("on_mm"), i + 1)
                dst = o_rs[:, 2 * i:2 * i + 2, :].rearrange("p a b -> p (a b)")
                act.activation(dst, ps[:, 4 + i, :], ACT.Ln, bias=eps_c[:, :], scale=1.0 / P).then_inc(s("on_rs"), 1)
            act.wait_ge(s("on_rs"), 4)
            act.activation(o_rs[:, :, :], o_rs[:, :, :], ACT.Exp, scale=-0.5).then_inc(s("on_rs"), 1)
            for i in range(8):
                act.wait_ge(s("pw_mm"), i + 1)
                act.activation(mixT[:, 8 + i, :], ps[:, i % 2, 0:T], ACT.Copy, scale=col_b[:, 120 + i:121 + i]
                               ).then_inc(s("mix_pool"), 1)
            for kt in range(KT):
                if kt < 8:
                    act.wait_ge(s("mix_lin"), 1)
                else:
                    act.wait_ge(s("mix_pool"), 8)
                act.copy(mix_hi[:, kt, :], mixT[:, kt, :]).then_inc(s("mixh"), 1)
            act.wait_ge(s("mix_lin"), 1)
            O2 = 2 * N_IN
            for n2 in range(O2, O2 + 2 * N_OUT):
                hi_split(act, n2)
                if n2 == O2 + KT + 2:
                    for i in range(4):
                        act.wait_ge(s("g1_mm"), i + 1)
                        act.copy(gate1[:, i * 512:(i + 1) * 512], ps[:, 4 + i, :]).then_inc(s("g1_ev"), 1)
            for t in range(2):
                act.wait_ge(s("x2_done"), 8)
                act.activation(sq2[:, t, :], x2[:, t, :], ACT.Square, accum_out=ssq[:, t:t + 1]
                               ).then_inc(s("sq2_done"), 1)
            act.wait_ge(s("sq2_done"), 2)
            act.activation(rms[:, 0:2], ssq[:, 0:2], ACT.Ln, bias=eps_c[:, :], scale=1.0 / D).then_inc(s("m2"), 1)
            act.wait_ge(s("m2"), 1)
            act.activation(rms[:, 0:2], rms[:, 0:2], ACT.Exp, scale=-0.5).then_inc(s("rms2"), 1)
            for kt in range(KT):
                act.wait_ge(s("mod2"), kt + 1)
                act.copy(xn2_hi[:, kt, :], xT2[:, kt, :]).then_inc(s("xn2h"), 1)
            H0 = 2 * (N_IN + N_OUT)

            def mlp_hi(it, k, h0, per):
                n2 = h0 + k
                if k % 2 == 0:
                    act.wait_ge(raw_in[(n2 // 2) % NRAW], it * (8 * per // NRAW) + 16 * (n2 // 2 // NRAW + 1))
                act.wait_ge(s("w_used"), it * per + n2 - NHL + 1 - 2 * N_IN)
                act.activation(w_hi[:, n2 % NHL, :],
                               raw[:, (n2 // 2) % NRAW, (n2 % 2) * HALF:(n2 % 2 + 1) * HALF],
                               ACT.Copy).then_inc(s("hi_done"), 1)

            def up_act(it, ahead):
                for k in range(16):
                    if k < ahead:
                        mlp_hi(it, k + 3, H0, 16)
                    if k % 8 == 7:
                        for i in range(2):
                            bank = 2 * (k // 8) + i
                            f0 = 2 * bank
                            act.wait_ge(s("w_used"), it * 16 + H0 - 2 * N_IN + k + 1)
                            act.activation(hT[:, ds(it * 8 + f0, 2), :].rearrange("p a b -> p (a b)"),
                                           ps[:, bank, :], ACT.Relu).then_inc(s("relu_a"), 1)

            act.wait_ge(s("xn2l"), KT)
            for k in range(3):
                mlp_hi(0, k, H0, 16)
            with act.Fori(0, 7) as it:
                up_act(it, 16)
            up_act(7, 13)
            for i in range(4):
                act.wait_ge(s("g2_mm"), i + 1)
                act.copy(gate2[:, i * 512:(i + 1) * 512], ps[:, 4 + i, :]).then_inc(s("g2_ev"), 1)
            E0 = H0 + 2 * N_UP
            act.wait_ge(s("relu_v"), 32)
            for ch in range(2):
                with act.Fori(0, 8) as it:
                    for k in range(8):
                        mlp_hi(it, k, E0 + 64 * ch, 8)
                        act.copy(h_hi[:, k % 4, :], hT[:, ds(it * 8 + k, 1), :].rearrange("p a b -> p (a b)")
                                 ).then_inc(s("hh"), 1)
            for t in range(2):
                act.wait_ge(s("fin_a"), 8)
                act.activation(sq2[:, t, :], x2[:, t, :], ACT.Square, accum_out=ssq[:, 2 + t:3 + t]
                               ).then_inc(s("sq2_done"), 1)
            act.wait_ge(s("sq2_done"), 4)
            act.activation(rms[:, 2:4], ssq[:, 2:4], ACT.Ln, bias=eps_c[:, :], scale=1.0 / D).then_inc(s("m2"), 1)
            act.wait_ge(s("m2"), 2)
            act.activation(rms[:, 2:4], rms[:, 2:4], ACT.Exp, scale=-0.5).then_inc(s("rms2"), 1)

        @block.vector
        def _(dve):
            steps = [0]

            def step(ins, wait=True):
                steps[0] += 1
                ins.then_inc(s("dve_step"), 1)
                dve.wait_ge(s("dve_step"), steps[0])

            dve.wait_ge(s("rowsT"), 1)
            step(dve.tensor_copy(col_a[:, :, :], ps[:, 6, 0:P].rearrange("p (a b) -> p a b", a=8)))
            step(dve.tensor_copy(col_b[:, :], ps[:, 6, P:2 * P]))
            dve.tensor_scalar(col_a[:, 5, :], col_a[:, 5, :], 1.0, None, ALU.add)
            dve.tensor_scalar(col_a[:, 7, :], col_a[:, 7, :], 1.0, None, ALU.add).then_inc(s("cols_dve"), 1)
            dve.wait_ge(s("wab_h"), 1)
            dve.tensor_tensor(wab_lo[:, :, :], wab_raw[:, :, :], wab_hi[:, :, :].bitcast(F32), ALU.subtract
                              ).then_inc(s("wab_l"), 1)
            dve.wait_ge(s("rms_done"), 1)
            for t in range(NT):
                dve.tensor_scalar(x_nat[:, t, :], x_nat[:, t, :], rms[:, t:t + 1], None, ALU.mult
                                  ).then_inc(s("xs_done"), 1)
            for kt in range(1, KT, 2):
                dve.wait_ge(s("xt_mm"), kt + 1)
                dve.tensor_copy(xT[:, kt, :], ps[:, kt % 4, :]).then_inc(s("xt_dve"), 1)

            def modulation(b):
                dve.wait_ge(s("ada_pe"), 8 * (b + 1))
                kb = slice(BK * b, BK * b + BK)
                sums = ps[:, 4, 0:16].rearrange("p (s k j) -> p s k j", s=2, j=2)
                step(dve.tensor_tensor(scale1[:, kb, :], sums[:, 1], bc_in(col_a[:, 5, kb], 2), ALU.add))
                dve.tensor_tensor(shift1[:, kb, :], sums[:, 0], bc_in(col_a[:, 4, kb], 2), ALU.add
                                  ).then_inc(s("modc_done"), 1)
                step(dve.tensor_tensor(scale1[:, kb, :], scale1[:, kb, :], bc_in(col_a[:, 2, kb], 2), ALU.mult))
                if b == 0:
                    dve.wait_ge(s("xt_act"), KT // 2)
                for kt in range(BK * b, BK * b + BK):
                    for j in range(2):
                        ins = dve.tensor_scalar(xT[:, kt, j * T:(j + 1) * T], xT[:, kt, j * T:(j + 1) * T],
                                                scale1[:, kt, j:j + 1], shift1[:, kt, j:j + 1], ALU.mult, ALU.add)
                    ins.then_inc(s("mod_done"), 1)

            def evac_in(m):
                both, u, hb = IN_UNITS[m // 2 % NU][1], m // 2 % NU, m % 2
                for i, no in enumerate(PLAN[m]):
                    dve.wait_ge(s("pj"), no + 1)
                    if m < 2 * HB:
                        dve.wait_ge(s("pj_act"), N0)
                    else:
                        dve.wait_ge(s("pj_dve"), PLAN[m - HB][i] - N0 + 1)
                    a = acc_of(u, hb, i, both)
                    dve.tensor_tensor(a, a, ps[:, no % 4, :], ALU.add).then_inc(s("pj_dve"), 1)

            def ada_row(b, j):
                part_k, sl = 8 * (b % 2) + j, ada_slot[("row", b, j)]
                dve.wait_ge(ada_in[sl], 16 * ada_count[("row", b, j)])
                sc = cond[:, part_k, 0:1]
                if part_k == 0:
                    if b:
                        dve.wait_ge(s("red_mm"), 1)
                    ins = dve.tensor_scalar(ada_acc[:, :], ada[:, sl, :], sc, None, ALU.mult)
                else:
                    dve.wait_ge(s("ada_dve"), row_no(b, j) - 1)
                    ins = dve.scalar_tensor_tensor(out=ada_acc[:, :], in0=ada[:, sl, :], scalar=sc,
                                                   in1=ada_acc[:, :], op0=ALU.mult, op1=ALU.add)
                ins.then_inc(s("ada_dve"), 1)

            def reduced(i):
                dve.wait_ge(s("red_mm"), i + 1)
                if i == 0:
                    dve.tensor_tensor(shift2[:, :], ps[:, 7, 0:KT], col_a[:, 6, :], ALU.add).then_inc(s("red_ev"), 1)
                else:
                    dve.tensor_tensor(scale2[:, :], ps[:, 7, 0:KT], col_a[:, 7, :], ALU.add).then_inc(s("red_ev"), 1)
                    dve.wait_ge(s("red_ev"), 2)
                    step(dve.tensor_tensor(scale2[:, :], scale2[:, :], col_a[:, 3, :], ALU.mult))

            dve.wait_ge(s("cond_done"), 1)
            for b in range(NB):
                for m in range(HB):
                    n2 = HB * b + m
                    lo_split(dve, n2)
                    if n2 - 3 >= HB:
                        evac_in(n2 - 3)
                    if m == 2:
                        if b == 0:
                            modulation(0)
                        for kt in range(BK):
                            dve.wait_ge(s("xnh"), BK * b + kt + 1)
                            dve.tensor_tensor(xn_lo[:, kt, :], xT[:, BK * b + kt, :],
                                              xn_hi[:, kt, :].bitcast(F32), ALU.subtract).then_inc(s("xnl"), 1)
                    if m == 4 and b == 2:
                        reduced(0)
                    if m >= 2 and m % 2 == 0 and m <= 16:
                        ada_row(b, (m - 2) // 2)
                    if m == 18 and b < NB - 1:
                        modulation(b + 1)
            for m in range(NB * HB - 3, NB * HB):
                evac_in(m)
            reduced(1)
            dve.wait_ge(s("ab_done"), 1)
            dve.wait_ge(s("small_in"), 64)
            ab = ps[:, 5, 0:P].rearrange("p (t c) -> p t c", t=NT)
            wait_used(dve, 2 * N_IN - 1)
            dve.tensor_tensor(g_in[:, :, :], ab[:, :, 0:16], bc(dtb[:, :], NT), ALU.add).then_inc(s("gp"), 1)
            dve.tensor_copy(nbeta[:, :, :], ab[:, :, 16:32]).then_inc(s("gp"), 1)
            dve.wait_ge(s("gp"), 1)
            dve.scalar_tensor_tensor(out=g_t1[:, :, :], in0=g_in[:, :, :], scalar=-1.0, in1=g_in[:, :, :],
                                     op0=ALU.mult, op1=ALU.min).then_inc(s("gp"), 1)
            dve.wait_ge(s("pj_dve"), PJ_DVE)
            n = 0
            for i in range(24):
                dve.wait_ge(s("conv0"), i + 1)
                for k in (0, 1, 3, 4):
                    d = k - CONV_K // 2
                    a, e = max(0, -d), T - max(0, d)
                    if i < 16:
                        u = acc_kv[:, i, :].rearrange("p (s t) -> p s t", s=2)
                        o = cbuf[:, i % 2, :].rearrange("p (s t) -> p s t", s=2)
                        u, o = u[:, :, a + d:e + d], o[:, :, a:e]
                    else:
                        u, o = acc_x[:, i - 16, a + d:e + d], cbuf[:, i % 2, a:e]
                    if k:
                        dve.wait_ge(s("conv"), n)
                    n += 1
                    dve.scalar_tensor_tensor(out=o, in0=u, scalar=tap(i, k), in1=o, op0=ALU.mult, op1=ALU.add
                                             ).then_inc(s("conv"), 1)
            for h in range(NH):
                dve.wait_ge(s("vtr"), h + 1)
                dve.tensor_copy(acc_kv[:, 8 + h, :], ps[:, 2 + h % 2, :]).then_inc(s("vnat_done"), 1)
            dve.wait_ge(s("gp_act"), 4)
            step(dve.scalar_tensor_tensor(out=g_t1[:, :, :], in0=g_in[:, :, :], scalar=0.0, in1=g_t2[:, :, :],
                                          op0=ALU.max, op1=ALU.add))
            dve.scalar_tensor_tensor(out=g_log[:, :, :], in0=g_t1[:, :, :], scalar=-1.0, in1=bc(alog[:, :], NT),
                                     op0=ALU.mult, op1=ALU.mult).then_inc(s("gp"), 1)
            step(dve.tensor_scalar(beta[:, :, :], beta[:, :, :], 1.0, None, ALU.add))
            step(dve.reciprocal(beta[:, :, :], beta[:, :, :]))
            step(dve.tensor_scalar(nbeta[:, :, :], beta[:, :, :], -1.0, None, ALU.mult))
            dve.wait_ge(s("gc_mm"), 1)
            tot = ps[:, 4, 64:128].rearrange("p (t c) -> p t c", t=NT)
            dve.tensor_copy(gcum[:, :, :], ps[:, 4, 0:64].rearrange("p (t c) -> p t c", t=NT)).then_inc(s("gc_ev"), 1)
            dve.wait_ge(s("gc_ev"), 1)
            dve.tensor_tensor(e_tail[:, :, :], tot, gcum[:, :, :], ALU.subtract).then_inc(s("gc_ev"), 1)
            dve.tensor_copy(e_last[:, :, :], tot).then_inc(s("gc_ev"), 1)
            for j in range(12):
                dve.wait_ge(s("l2_rs"), 2 * j + 2)
                if j < 8:
                    dve.tensor_tensor(acc_kv[:, j, :], acc_kv[:, j, :], rsb[:, j % 2, :], ALU.mult
                                      ).then_inc(s("l2_done"), 1)
                else:
                    q2 = acc_x[:, 2 * (j - 8):2 * (j - 8) + 2, :].rearrange("p a c -> p (a c)")
                    dve.scalar_tensor_tensor(out=q2, in0=q2, scalar=float(P) ** -0.5, in1=rsb[:, j % 2, :],
                                             op0=ALU.mult, op1=ALU.mult).then_inc(s("l2_done"), 1)
            dve.wait_ge(s("gp_act"), 7)
            dve.tensor_scalar(neg_eg[:, :, :], neg_eg[:, :, :], -1.0, None, ALU.mult).then_inc(s("gp_sel"), 1)
            q4 = "p (t c) -> p t c"

            def kk_evac(h):
                dve.wait_ge(s("kk_mm"), 2 * h + 1)
                if h:
                    dve.wait_ge(s("am_pool"), 2 * h)
                dve.wait_ge(s("masks"), N_MASKS)
                for d, m in ((0, SU), (1, SL)):
                    dve.tensor_tensor(KK[:, d, :].rearrange(q4, t=4), ps[:, 6, :].rearrange(q4, t=4),
                                      bc(tri[:, m, :], 4), ALU.mult).then_inc(s("kk_ev"), 1)
                dve.wait_ge(s("kk_mm"), 2 * h + 2)
                for d, m in ((0, UI), (1, LI)):
                    dve.tensor_tensor(QK[:, d, :].rearrange(q4, t=2), ps[:, 7, 0:T].rearrange(q4, t=2),
                                      bc(tri[:, m, :], 2), ALU.mult).then_inc(s("kk_ev"), 1)

            def gb_evac(r):
                h, d = r // 2, r % 2
                dve.wait_ge(s("gb_mm"), r + 1)
                if r >= 2:
                    dve.wait_ge(s("t1_mm"), r - 1)
                for t in range(NCH):
                    cs = slice(t * P, (t + 1) * P)
                    dve.tensor_scalar(Eb[:, r % 2, cs], ps[:, gb_bank(r), cs], gcum[:, t, 8 * d + h:8 * d + h + 1],
                                      0.0, ALU.subtract, ALU.min).then_inc(s("gb_ev"), 1)

            def mn_evac(r):
                h, d = r // 2, r % 2
                dve.wait_ge(s("t1_mm"), r + 1)
                if r:
                    dve.wait_ge(s("t2_mm"), r)
                    dve.wait_ge(s("x0"), 2 * r)
                dve.tensor_tensor(Mn[:, :].rearrange(q4, t=4), ps[:, t1_bank(r), :].rearrange(q4, t=4),
                                  bc_in(nbeta[:, :, 8 * d + h], P), ALU.mult).then_inc(s("mn_ev"), 1)

            def start_inverse(r, which):
                d, g2, q = r % 2, (r // 4) % 2, r % 4
                if which == 0:
                    dst, src, m = Xb[:, g2, q, :], Mn[:, :], (m_low, m_up)[d]
                    name = "x0"
                    if r >= 8:
                        dve.wait_ge(s("x_upd"), inverted(r - 8 + 3 - r % 4))
                    dve.wait_ge(s("mn_ev"), r + 1)
                else:
                    dst, src, m = XT[:, r, :], MT[:, g2, q, :], (m_up, m_low)[d]
                    name = "xt0"
                    dve.wait_ge(s("mt_ev"), r + 1)
                dst, src = dst.rearrange(q4, t=4), src.rearrange(q4, t=4)
                dve.tensor_tensor(dst, src, bc(m[:, 0, :], 4), ALU.mult).then_inc(s(name), 1)
                dve.wait_ge(s(name), 2 * r + 1)
                dve.tensor_tensor(dst, dst, bc(ident[:, :], 4), ALU.add).then_inc(s(name), 1)

            def p_evac(G, i):
                no, lv, d = 24 * G + i, 1 + i // 4, i % 2
                dve.wait_ge(s("p_mm"), no + 1)
                if no >= 2:
                    dve.wait_ge(s("y_mm"), no - 1)
                dve.tensor_tensor(Pb[:, no % 2, :].rearrange(q4, t=4), ps[:, no % 2, :].rearrange(q4, t=4),
                                  bc((m_low, m_up)[d][:, lv, :], 4), ALU.mult).then_inc(s("p_ev"), 1)

            def x_update(G, i):
                no, lv, q = 24 * G + i, 1 + i // 4, i % 4
                r = 4 * G + q
                h, d = r // 2, r % 2
                dve.wait_ge(s("y_mm"), no + 1)
                xt = XT[:, r, :]
                if lv < LEVELS:
                    xx = Xb[:, G % 2, q, :]
                    dve.tensor_tensor(xx, xx, ps[:, 2 + no % 2, :], ALU.add)
                    dve.tensor_tensor(xt, xt, ps[:, 4 + no % 2, :], ALU.add).then_inc(s("x_upd"), 1)
                else:
                    step(dve.tensor_tensor(xt, xt, ps[:, 4 + no % 2, :], ALU.add))
                    xt = xt.rearrange(q4, t=4)
                    dve.tensor_tensor(xt, xt, bc_in(beta[:, :, 8 * d + h], P), ALU.mult).then_inc(s("x_upd"), 1)

            dve.wait_ge(s("l2_done"), 12)
            for G in range(-1, 4):
                for i in range(26):
                    if G >= 0:
                        if i < 24:
                            p_evac(G, i)
                        if i >= 2:
                            x_update(G, i - 2)
                    if G < 3:
                        q, j = i // 6, i % 6
                        r = 4 * (G + 1) + q
                        if j == 0 and q:
                            start_inverse(r - 1, 1)
                        if q < 4:
                            if j == 0 and q % 2 == 0:
                                kk_evac(r // 2)
                            if j == 1:
                                gb_evac(r)
                            if j == 4:
                                mn_evac(r)
                            if j == 5:
                                start_inverse(r, 0)
            for n in range(NCHAIN):
                h, d = n // 2, 1 - n % 2
                dve.wait_ge(s("er_exp"), n + 1)
                dst = qd_b[:, h, :] if d else acc_x[:, h, :]
                if d == 0:
                    dve.wait_ge(s("qd"), n)
                else:
                    dve.wait_ge(s("x_upd"), inverted(NCHAIN - 1))
                dve.tensor_tensor(dst, acc_x[:, h, :], eg_row[:, n % 2, :], ALU.mult).then_inc(s("qd"), 1)
            for st in range(4):
                for g in range(4):
                    if st:
                        dve.wait_ge(s("ks_mm"), 4 * (st - 1) + g + 1)
                        for q in range(4):
                            h, d = 2 * g + q // 2, q % 2
                            t = chunk_at(st, d)
                            ins = dve.scalar_tensor_tensor(
                                out=rb[:, g, q * P:(q + 1) * P], in0=ps[:, g, q * P:(q + 1) * P],
                                scalar=neg_eg[:, t, 8 * d + h:8 * d + h + 1], in1=acc_kv[:, 8 + h, t * P:(t + 1) * P],
                                op0=ALU.mult, op1=ALU.add)
                        ins.then_inc(s("r_ev"), 1)
                for g in range(4):
                    dve.wait_ge(s("vn_mm"), 4 * st + g + 1)
                    if st:
                        dve.wait_ge(s("vt_ev"), 4 * (4 * (st - 1) + g + 1))
                    dve.tensor_copy(vn[:, g, :], ps[:, g, :]).then_inc(s("vn_ev"), 1)
                if st == 3:
                    break
                for g in range(4):
                    dve.wait_ge(s("su_mm"), 4 * st + g + 1)
                    if st == 0:
                        dve.tensor_copy(Sb[:, 4 * g:4 * g + 4, :].rearrange("p a b -> p (a b)"), ps[:, g, :]
                                        ).then_inc(s("s_ev"), 1)
                        continue
                    dve.wait_ge(s("s_ev"), 4 * (st - 1) + g + 1)
                    for q in range(4):
                        h, d = 2 * g + q // 2, q % 2
                        t = chunk_at(st, d)
                        ins = dve.scalar_tensor_tensor(
                            out=Sb[:, 4 * g + q, :], in0=Sb[:, 4 * g + q, :],
                            scalar=e_last[:, t, 8 * d + h:8 * d + h + 1], in1=ps[:, g, q * P:(q + 1) * P],
                            op0=ALU.mult, op1=ALU.add)
                    ins.then_inc(s("s_ev"), 1)
            dve.wait_ge(s("o_mm"), 1)
            for i in range(4):
                dve.tensor_copy(o_sb[:, 2 * i:2 * i + 2, :].rearrange("p a b -> p (a b)"), ps[:, 4 + i, :]
                                ).then_inc(s("o_ev"), 1)
            dve.wait_ge(s("o_sqd"), 1)
            dve.wait_ge(s("o_ev"), 4)
            dve.wait_ge(s("zsilu"), 1)
            step(dve.scalar_tensor_tensor(out=o_sb[:, :, :], in0=o_sb[:, :, :], scalar=onorm[:, 0:1],
                                          in1=acc_x[:, 8:16, :], op0=ALU.mult, op1=ALU.mult))
            dve.wait_ge(s("on_rs"), 5)
            dve.tensor_tensor(mixT[:, 0:8, :], o_sb[:, :, :], o_rs[:, :, :], ALU.mult).then_inc(s("mix_lin"), 1)
            for kt in range(KT):
                dve.wait_ge(s("mixh"), kt + 1)
                dve.tensor_tensor(mix_lo[:, kt, :], mixT[:, kt, :], mix_hi[:, kt, :].bitcast(F32), ALU.subtract
                                  ).then_inc(s("mixl"), 1)

            def y_evac(ch, i):
                tk, cc = i // 2, i % 2
                n_y = 4 * ch + i
                cs = slice(ch * 1024 + cc * 512, ch * 1024 + (cc + 1) * 512)
                wait_used(dve, 2 * N_IN + KT * (ch + 1) - 1)
                dve.wait_ge(s("g1_ev"), 4)
                if n_y >= 2:
                    dve.wait_ge(s("x2_done"), n_y - 1)
                step(dve.tensor_tensor(yt[:, n_y % 2, :], ps[:, 4 * ch + i, :], gate1[:, cs], ALU.mult))
                dve.wait_ge(s("xres_in"), 16)
                dve.tensor_tensor(x2[:, tk, cs], x2[:, tk, cs], yt[:, n_y % 2, :], ALU.add).then_inc(s("x2_done"), 1)

            O2 = 2 * N_IN
            for j in range(2 * N_OUT):
                lo_split(dve, O2 + j)
                if j < KT:
                    if j == 0:
                        dve.wait_ge(s("g1_b"), 16)
                    else:
                        dve.wait_ge(s("ada_dve"), 32 + j)
                    sl = j % 2
                    dve.wait_ge(gate_in[sl], 16 * (sl + j // 2 + 1))
                    dve.scalar_tensor_tensor(out=g1_acc[:, :], in0=ada[:, sl, :], scalar=cond[:, j, 0:1],
                                             in1=g1_acc[:, :], op0=ALU.mult, op1=ALU.add).then_inc(s("ada_dve"), 1)
                if KT + 2 <= j < KT + 6:
                    y_evac(0, j - KT - 2)
            for i in range(4):
                y_evac(1, i)
            dve.wait_ge(s("rms2"), 1)
            for t in range(2):
                dve.tensor_scalar(xs2[:, t, :], x2[:, t, :], rms[:, t:t + 1], None, ALU.mult).then_inc(s("xs2_done"), 1)
            for kt in range(KT):
                dve.wait_ge(s("t3_mm"), kt // 2 + 1)
                dve.tensor_scalar(xT2[:, kt, :], ps[:, (kt // 2) % 4, (kt % 2) * T:(kt % 2 + 1) * T],
                                  scale2[:, kt:kt + 1], shift2[:, kt:kt + 1], ALU.mult, ALU.add).then_inc(s("mod2"), 1)
            for kt in range(KT):
                dve.wait_ge(s("xn2h"), kt + 1)
                dve.tensor_tensor(xn2_lo[:, kt, :], xT2[:, kt, :], xn2_hi[:, kt, :].bitcast(F32), ALU.subtract
                                  ).then_inc(s("xn2l"), 1)
            H0 = 2 * (N_IN + N_OUT)
            E0 = H0 + 2 * N_UP

            def mlp_lo(it, k, h0, per):
                n2 = h0 + k
                hs = slice((n2 % 2) * HALF, (n2 % 2 + 1) * HALF)
                dve.wait_ge(s("hi_done"), it * per + n2 + 1)
                dve.tensor_tensor(w_lo[:, n2 % NHL, :], raw[:, (n2 // 2) % NRAW, hs],
                                  w_hi[:, n2 % NHL, :].bitcast(F32), ALU.subtract).then_inc(s("lo_done"), 1)

            def up_dve(it, ahead):
                for k in range(16):
                    if k < ahead:
                        mlp_lo(it, k + 3, H0, 16)
                    if k % 8 == 4:
                        j = k // 8
                        dve.wait_ge(gate_in[j], it * 16 + 16 * (8 + j + 1))
                        dve.wait_ge(s("ada_dve"), it * 2 + 48 + j)
                        dve.scalar_tensor_tensor(out=g2_acc[:, :], in0=ada[:, j, :],
                                                 scalar=cond[:, ds(it * 2 + j, 1), 0], in1=g2_acc[:, :],
                                                 op0=ALU.mult, op1=ALU.add).then_inc(s("ada_dve"), 1)
                    if k % 8 == 7:
                        for i in range(2):
                            bank = 2 * (k // 8) + i
                            hh = hT[:, ds(it * 8 + 2 * bank, 2), :].rearrange("p a b -> p (a b)")
                            dve.wait_ge(s("relu_a"), it * 4 + bank + 1)
                            dve.tensor_tensor(hh, hh, hh, ALU.mult).then_inc(s("relu_v"), 1)

            dve.wait_ge(s("g2_b"), 16)
            for k in range(3):
                mlp_lo(0, k, H0, 16)
            with dve.Fori(0, 7) as it:
                up_dve(it, 16)
            up_dve(7, 13)

            def z_evac(ch):
                wait_used(dve, E0 + 64 * (ch + 1) - 1)
                dve.wait_ge(s("g2_ev"), 4)
                for i in range(4):
                    tk, cc = i // 2, i % 2
                    cs = slice(ch * 1024 + cc * 512, ch * 1024 + (cc + 1) * 512)
                    step(dve.tensor_tensor(yt2[:, i % 2, :], ps[:, 4 * ch + i, :], gate2[:, cs], ALU.mult))
                    dve.tensor_tensor(x2[:, tk, cs], x2[:, tk, cs], yt2[:, i % 2, :], ALU.add).then_inc(s("fin_a"), 1)

            for ch in range(2):
                with dve.Fori(0, 8) as it:
                    for k in range(8):
                        mlp_lo(it, k, E0 + 64 * ch, 8)
                        dve.wait_ge(s("hh"), it * 8 + 64 * ch + k + 1)
                        dve.tensor_tensor(h_lo[:, k % 4, :], hT[:, ds(it * 8 + k, 1), :].rearrange("p a b -> p (a b)"),
                                          h_hi[:, k % 4, :].bitcast(F32), ALU.subtract).then_inc(s("hl"), 1)
                z_evac(ch)
            dve.wait_ge(s("fin_in"), 16)
            dve.wait_ge(s("rms2"), 2)
            for t in range(2):
                dve.scalar_tensor_tensor(out=x2[:, t, :], in0=x2[:, t, :], scalar=rms[:, 2 + t:3 + t],
                                         in1=fin_w[:, :], op0=ALU.mult, op1=ALU.mult).then_inc(s("fin_c"), 1)

        @block.tensor
        def _(pe):
            mm = pe.matmul

            def three(o, xh, xl, wh, wl, start, stop, x_stationary):
                pairs = ((xh, wh), (xh, wl), (xl, wh)) if x_stationary else ((wh, xh), (wh, xl), (wl, xh))
                for i, (l, r) in enumerate(pairs):
                    ins = mm(o, l, r, start=start and i == 0, stop=stop and i == 2, skip_group_check=True)
                return ins

            pe.wait_ge(s("const_done"), 1)
            pe.wait_ge(s("rows_in"), 160)
            pe.transpose(ps[:, 6, 0:P], rows_a[:, :], ident[:, :])
            pe.transpose(ps[:, 6, P:2 * P], rows_b[:, :], ident[:, :]).then_inc(s("rowsT"), 1)
            pe.wait_ge(s("xs_done"), NT)
            for kt in range(KT):
                if kt >= 4:
                    pe.wait_ge(s("xt_dve" if kt % 2 else "xt_act"), (kt - 4) // 2 + 1)
                for t in range(NT):
                    ins = pe.transpose(ps[:, kt % 4, t * P:(t + 1) * P], x_nat[:, t, kt * P:(kt + 1) * P], ident[:, :])
                ins.then_inc(s("xt_mm"), 1)

            def ada_mod(b, j):
                it = ("mod", b, j)
                pe.wait_ge(ada_in[ada_slot[it]], 16 * ada_count[it])
                if j == 0 and b:
                    pe.wait_ge(s("modc_done"), b)
                part, g = j // 4, j % 4
                for kk in range(4):
                    for ct in range(4):
                        o = ps[:, 4, 8 * part + 2 * ct:8 * part + 2 * ct + 2]
                        c0 = kk * 512 + ct * P
                        ins = mm(o, ada[:, ada_slot[it], c0:c0 + P], cond[:, 4 * g + kk, :],
                                 start=(j == 0 and kk == 0 and ct == 0), stop=(g == 3 and kk == 3),
                                 skip_group_check=True)
                ins.then_inc(s("ada_pe"), 1)

            pe.wait_ge(s("cond_done"), 1)
            for j in range(8):
                ada_mod(0, j)

            def in_half(b, m):
                n2 = HB * b + m
                u, hb = m // 2, m % 2
                both = IN_UNITS[u][1]
                wh = w_hi[:, n2 % NHL, :].rearrange("p (k c) -> p k c", k=4)
                wl = w_lo[:, n2 % NHL, :].rearrange("p (k c) -> p k c", k=4)
                nn = 2 * T if both else T
                pe.wait_ge(s("lo_done"), n2 + 1)
                for ct in range(2):
                    no = PLAN[n2][ct if both else 0]
                    if no >= 4 and (both or ct == 0):
                        if no - 4 < N0:
                            pe.wait_ge(s("pj_act"), no - 4 + 1)
                        else:
                            pe.wait_ge(s("pj_dve"), no - 4 - N0 + 1)
                    o = ps[:, no % 4, :] if both else ps[:, no % 4, ct * T:(ct + 1) * T]
                    cs = slice(ct * P, (ct + 1) * P)
                    for k in range(BK):
                        ins = three(o, xn_hi[:, k, 0:nn], xn_lo[:, k, 0:nn], wh[:, k, cs], wl[:, k, cs],
                                    k == 0 and (both or ct == 0), k == BK - 1, False)
                    if both and ct == 0:
                        ins.then_inc(s("pj"), 1)
                return ins

            for b in range(NB):
                if b == 0:
                    pe.wait_ge(s("wab_l"), 1)
                    pe.wait_ge(s("xt_act"), KT // 2)
                    pe.wait_ge(s("xt_dve"), KT // 2)
                for k in range(BK):
                    pe.wait_ge(s("xnl"), BK * b + k + 1)
                    for t in range(NT):
                        ts = slice(t * P, (t + 1) * P)
                        ins = three(ps[:, 5, t * 32:(t + 1) * 32], xn_hi[:, k, ts], xn_lo[:, k, ts],
                                    wab_hi[:, BK * b + k, :], wab_lo[:, BK * b + k, :],
                                    b == 0 and k == 0 and t == 0, b == NB - 1 and k == BK - 1, True)
                if b == NB - 1:
                    ins.then_inc(s("ab_done"), 1)
                for m in range(HB):
                    in_half(b, m).then_inc(s("pj"), 1)
                    if b < NB - 1 and m % 2 == 1 and m < 16:
                        ada_mod(b + 1, m // 2)
                if b % 2 == 1:
                    pe.wait_ge(s("ada_dve"), 8 * (b + 1))
                    if b == 3:
                        pe.wait_ge(s("red_ev"), 1)
                    for kt in range(KT):
                        ins = mm(ps[:, 7, kt:kt + 1], ada_acc[:, kt * P:(kt + 1) * P], ones[:, 0:1],
                                 start=True, stop=True)
                    ins.then_inc(s("red_mm"), 1)
            pe.wait_ge(s("xt_act"), KT // 2)
            for h in range(NH):
                pe.wait_ge(s("silu"), 8 + h + 1)
                pe.wait_ge(s("pj_dve"), PJ_DVE)
                if h >= 2:
                    pe.wait_ge(s("vnat_done"), h - 1)
                for t in range(NCH):
                    ts = slice(t * P, (t + 1) * P)
                    ins = pe.transpose(ps[:, 2 + h % 2, ts], acc_kv[:, 8 + h, ts], ident[:, :])
                ins.then_inc(s("vtr"), 1)
            pe.wait_ge(s("masks"), N_MASKS)
            pe.wait_ge(s("gp"), 4)
            gc = ps[:, 4, 0:64].rearrange("p (t c) -> p t c", t=NT)
            mm(gc[:, :, 0:8], tri[:, UI, :], g_log[:, :, 0:8], start=True, stop=True)
            mm(gc[:, :, 8:16], tri[:, LI, :], g_log[:, :, 8:16], start=True, stop=True)
            mm(ps[:, 4, 64:128], ones[:, :], g_log[:, :, :].rearrange("p t c -> p (t c)"), start=True, stop=True
               ).then_inc(s("gc_mm"), 1)
            pe.wait_ge(s("gc_ev"), 1)
            for t in range(NT):
                ins = pe.transpose(ps[0:16, 5, t * P:(t + 1) * P], gcum[:, t, :], ident[:, :])
            ins.then_inc(s("gcT_mm"), 1)
            for j in range(12):
                pe.wait_ge(s("l2_sq"), j + 1)
                if j >= 2:
                    pe.wait_ge(s("l2_rs"), 2 * (j - 2) + 1)
                mm(ps[:, j % 2, :], ones[:, :], sqb[:, j % 2, :], start=True, stop=True).then_inc(s("l2_mm"), 1)
            pe.wait_ge(s("l2_done"), 12)
            pe.wait_ge(s("gcT_ev"), 1)
            pe.wait_ge(s("vnat_done"), NH)
            pe.wait_ge(s("red_ev"), 2)

            def cs(t):
                return slice(t * P, (t + 1) * P)

            def kk_products(h):
                if h:
                    pe.wait_ge(s("mn_ev"), 2 * h)
                for t in range(NCH):
                    k = acc_kv[:, h, cs(t)]
                    ins = mm(ps[:, 6, cs(t)], k, k, start=True, stop=True)
                ins.then_inc(s("kk_mm"), 1)
                if h:
                    pe.wait_ge(s("mt_ev"), 2 * h)
                for t in range(2):
                    ins = mm(ps[:, 7, cs(t)], acc_kv[:, h, cs(t)], acc_x[:, h, cs(t)], start=True, stop=True)
                ins.then_inc(s("kk_mm"), 1)

            def decay_rows(r):
                h, d = r // 2, r % 2
                if d == 0:
                    pe.wait_ge(s("kk_ev"), 4 * h + 2)
                else:
                    pe.wait_ge(s("mn_ev"), r)
                mm(ps[:, gb_bank(r), :], sel[:, 8 * d + h, :], gcT[:, :], start=True, stop=True
                   ).then_inc(s("gb_mm"), 1)

            def turn1(r):
                pe.wait_ge(s("am_pool"), r + 1)
                if r % 2 == 0:
                    pe.wait_ge(s("kk_ev"), 4 * (r // 2) + 4)
                else:
                    pe.wait_ge(s("mt_ev"), r)
                for t in range(NCH):
                    ins = pe.transpose(ps[:, t1_bank(r), cs(t)], Eb[:, r % 2, cs(t)], ident[:, :])
                ins.then_inc(s("t1_mm"), 1)

            def turn2(r):
                pe.wait_ge(s("mn_ev"), r + 1)
                pe.wait_ge(s("gb_ev"), 4 * (r + 1))
                for t in range(NCH):
                    ins = pe.transpose(ps[:, t2_bank(r), cs(t)], Mn[:, cs(t)], ident[:, :])
                ins.then_inc(s("t2_mm"), 1)

            def p_products(G, i):
                no, q = 24 * G + i, i % 4
                if i < 4:
                    pe.wait_ge(s("x0"), 2 * (4 * G + q + 1))
                    pe.wait_ge(s("xt0"), 2 * (4 * G + q + 1))
                else:
                    pe.wait_ge(s("x_upd"), no - 4 + 1)
                if no >= 2:
                    pe.wait_ge(s("p_ev"), no - 1)
                for t in range(NCH):
                    ins = mm(ps[:, no % 2, cs(t)], MT[:, G % 2, q, cs(t)], Xb[:, G % 2, q, cs(t)], start=True, stop=True)
                ins.then_inc(s("p_mm"), 1)

            def y_products(G, i):
                no, q, lv = 24 * G + i, i % 4, 1 + i // 4
                pe.wait_ge(s("p_ev"), no + 1)
                if no >= 2:
                    pe.wait_ge(s("x_upd"), no - 1)
                for t in range(NCH):
                    if lv < LEVELS:
                        mm(ps[:, 2 + no % 2, cs(t)], XT[:, 4 * G + q, cs(t)], Pb[:, no % 2, cs(t)], start=True, stop=True)
                for t in range(NCH):
                    ins = mm(ps[:, 4 + no % 2, cs(t)], Pb[:, no % 2, cs(t)], XT[:, 4 * G + q, cs(t)], start=True, stop=True)
                ins.then_inc(s("y_mm"), 1)

            for G in range(-1, 4):
                for i in range(26):
                    if G >= 0:
                        if i < 24:
                            p_products(G, i)
                        if i >= 2:
                            y_products(G, i - 2)
                    if G < 3:
                        q, j = i // 6, i % 6
                        r = 4 * (G + 1) + q
                        if q < 4:
                            if j == 0 and q % 2 == 0:
                                kk_products(r // 2)
                            if j == 1:
                                decay_rows(r)
                            if j == 4:
                                turn1(r)
                            if j == 5:
                                turn2(r)
            pe.wait_ge(s("x_upd"), inverted(NCHAIN - 1))
            for n in range(NCHAIN):
                h, d = n // 2, 1 - n % 2
                if n >= 2:
                    pe.wait_ge(s("er_exp"), n - 1)
                mm(ps[:, n % 2, 0:T], sel[:, 8 * d + h, :], gcT[:, 0:T], start=True, stop=True).then_inc(s("er_mm"), 1)
                if n < NH:
                    if n >= 2:
                        pe.wait_ge(s("kn_ev"), n - 1)
                    for t in range(NCH):
                        ins = pe.transpose(ps[:, 2 + n % 2, cs(t)], acc_kv[:, n, cs(t)], ident[:, :])
                    ins.then_inc(s("ktr"), 1)
            pe.wait_ge(s("kn_ev"), NH)
            pe.wait_ge(s("er_exp"), NCHAIN)
            pe.wait_ge(s("qd"), NCHAIN)
            for st in range(4):
                for g in range(4):
                    if st:
                        pe.wait_ge(s("s_ev"), 4 * (st - 1) + g + 1)
                        for q in range(4):
                            h, d = 2 * g + q // 2, q % 2
                            ins = mm(ps[:, g, cs(q)], acc_kv[:, h, cs(chunk_at(st, d))], Sb[:, 4 * g + q, :],
                                     start=True, stop=True)
                        ins.then_inc(s("ks_mm"), 1)
                for g in range(4):
                    if st:
                        pe.wait_ge(s("r_ev"), 4 * (st - 1) + g + 1)
                    for q in range(4):
                        h, d = 2 * g + q // 2, q % 2
                        t = chunk_at(st, d)
                        rhs = rb[:, g, cs(q)] if st else acc_kv[:, 8 + h, cs(t)]
                        ins = mm(ps[:, g, cs(q)], XT[:, 4 * g + q, cs(t)], rhs, start=True, stop=True)
                    ins.then_inc(s("vn_mm"), 1)
                for g in range(4):
                    pe.wait_ge(s("vn_ev"), 4 * st + g + 1)
                    if st >= 2:
                        for q in range(4):
                            h, d = 2 * g + q // 2, q % 2
                            t = chunk_at(st, d)
                            o = ps[:, 4 + g, (q // 2) * T + t * P:(q // 2) * T + (t + 1) * P]
                            qd = qd_b[:, h, cs(t)] if d else acc_x[:, h, cs(t)]
                            mm(o, Sb[:, 4 * g + q, :], qd, start=(st == 2 and q == 0), stop=False, skip_group_check=True)
                            ins = mm(o, vn[:, g, cs(q)], At[:, 4 * g + q, cs(t)], start=False, stop=(st == 3),
                                     skip_group_check=True)
                    if st < 3:
                        pe.wait_ge(s("vt_ev"), 4 * (4 * st + g + 1))
                        for q in range(4):
                            h, d = 2 * g + q // 2, q % 2
                            ins = mm(ps[:, g, cs(q)], k_nat[:, h, chunk_at(st, d), :], vt[:, g, cs(q)],
                                     start=True, stop=True)
                        ins.then_inc(s("su_mm"), 1)
            ins.then_inc(s("o_mm"), 1)
            pe.wait_ge(s("o_sqd"), 1)
            for i in range(4):
                mm(ps[:, 4 + i, :], ones[:, :], o_sq[:, 2 * i:2 * i + 2, :].rearrange("p a b -> p (a b)"),
                   start=True, stop=True).then_inc(s("on_mm"), 1)
            pe.wait_ge(gate_in[1], 16)
            for i in range(8):
                g, o_ = i // 2, i % 2
                pe.wait_ge(s("pool_d"), g + 1)
                if i >= 2:
                    pe.wait_ge(s("mix_pool"), i - 1)
                for it in range(2):
                    c0 = (2 * g + it) * 256 + o_ * P
                    ins = mm(ps[:, i % 2, 0:T], ada[:, 1, c0:c0 + P], acc_x[:, 16 + 2 * g + it, :],
                             start=(it == 0), stop=(it == 1))
                ins.then_inc(s("pw_mm"), 1)

            def wide_half(slot, xh, xl, bank0, start, stop):
                for tk in range(2):
                    for cc in range(2):
                        ws = slice(cc * 512, (cc + 1) * 512)
                        ts = slice(tk * P, (tk + 1) * P)
                        ins = three(ps[:, bank0 + 2 * tk + cc, :], xh[:, ts], xl[:, ts], w_hi[:, slot, ws],
                                    w_lo[:, slot, ws], start, stop, True)
                return ins

            pe.wait_ge(s("mix_pool"), 8)
            for ch in range(2):
                for kt in range(KT):
                    n2 = 2 * N_IN + KT * ch + kt
                    pe.wait_ge(s("mixl"), kt + 1)
                    pe.wait_ge(s("lo_done"), n2 + 1)
                    wide_half(n2 % NHL, mix_hi[:, kt, :], mix_lo[:, kt, :], 4 * ch, kt == 0, kt == KT - 1
                              ).then_inc(s("w_used"), 1)
                if ch == 0:
                    pe.wait_ge(s("ada_dve"), 48)
                    pe.wait_ge(s("on_rs"), 4)
                    for i in range(4):
                        mm(ps[:, 4 + i, :], ones[:, :], g1_acc[:, i * 512:(i + 1) * 512], start=True, stop=True
                           ).then_inc(s("g1_mm"), 1)
                    pe.wait_ge(s("g1_ev"), 4)
            pe.wait_ge(s("xs2_done"), 2)
            for i in range(8):
                if i >= 4:
                    pe.wait_ge(s("mod2"), 2 * (i - 4) + 2)
                for j in range(4):
                    kt, t = 2 * i + j // 2, j % 2
                    ins = pe.transpose(ps[:, i % 4, j * P:(j + 1) * P], xs2[:, t, kt * P:(kt + 1) * P], ident[:, :])
                ins.then_inc(s("t3_mm"), 1)
            H0 = 2 * (N_IN + N_OUT)
            E0 = H0 + 2 * N_UP

            def up_pe(it, first):
                for k in range(16):
                    cc, m = k // 8, k % 8
                    pe.wait_ge(s("lo_done"), it * 16 + H0 + k + 1)
                    if m == 0:
                        if first:
                            pe.wait_ge(s("xn2l"), KT)
                        else:
                            pe.wait_ge(s("relu_a"), it * 4 + 2 * cc + 2 - 4)
                    slot = (H0 + k) % NHL
                    for j in range(4):
                        o = ps[:, 2 * cc + j // 2, (j % 2) * T:(j % 2 + 1) * T]
                        for kk in range(2):
                            kt, ws = 2 * m + kk, slice(kk * 512 + j * P, kk * 512 + (j + 1) * P)
                            ins = three(o, xn2_hi[:, kt, :], xn2_lo[:, kt, :], w_hi[:, slot, ws], w_lo[:, slot, ws],
                                        m == 0 and kk == 0 and j % 2 == 0, m == 7 and kk == 1, False)
                    ins.then_inc(s("w_used"), 1)

            pe.wait_ge(s("mod2"), KT)
            up_pe(0, True)
            with pe.Fori(1, 8) as it:
                up_pe(it, False)
            pe.wait_ge(s("relu_a"), 32)
            pe.wait_ge(s("zr"), 1)
            pe.wait_ge(s("ada_dve"), 64)
            pe.wait_ge(s("x2_done"), 8)
            for i in range(4):
                mm(ps[:, 4 + i, :], ones[:, :], g2_acc[:, i * 512:(i + 1) * 512], start=True, stop=True
                   ).then_inc(s("g2_mm"), 1)
            for ch in range(2):
                if ch:
                    pe.wait_ge(s("g2_ev"), 4)
                for i in range(4):
                    mm(ps[:, 4 * ch + i, :], zero_r[:, 0:P], zero_r[:, :], start=True, stop=False, skip_group_check=True)
                with pe.Fori(0, 8) as it:
                    for k in range(8):
                        pe.wait_ge(s("lo_done"), it * 8 + E0 + 64 * ch + k + 1)
                        pe.wait_ge(s("hl"), it * 8 + 64 * ch + k + 1)
                        wide_half((E0 + k) % NHL, h_hi[:, k % 4, :], h_lo[:, k % 4, :], 4 * ch, False, False
                                  ).then_inc(s("w_used"), 1)


_INS = ['x', 'c', 'ctx', 'c_ctx', 'w_ada', 'b_ada', 'norm1_w', 'norm2_w', 'w_in', 'conv_w', 'a_log', 'dt_bias',
        'onorm_w', 'pool_w', 'pool_scale', 'w_out', 'w_up', 'w_down', 'final_norm_w']
_OUTS = [((1, T, D), 'float32')]


def kernel(**inputs):
    import numpy as _np
    import concourse.bacc as _bacc
    from concourse import mybir as _mybir
    from concourse.bass_utils import run_bass_kernel_spmd as _run

    nc = _bacc.Bacc("TRN2", target_bir_lowering=False, num_devices=1)
    arrays, args = {}, []
    for name in _INS:
        a = _np.ascontiguousarray(inputs[name])
        arrays[f"in_{name}_dram"] = a
        args.append(nc.dram_tensor(f"in_{name}_dram", a.shape, _mybir.dt.from_np(a.dtype), kind="ExternalInput").ap())
    for i, (shape, dtype) in enumerate(_OUTS):
        dt = _mybir.dt.from_np(_np.dtype(dtype))
        args.append(nc.dram_tensor(f"out_{i}_dram", shape, dt, kind="ExternalOutput").ap())
    build(nc, *args)
    r = _run(nc, [arrays], core_ids=[0])
    return r.results[0]["out_0_dram"]
```

```python
from contextlib import ExitStack

import concourse.bass as bass
from concourse import mybir
from concourse.bass import ds

F32 = mybir.dt.float32
F32R = mybir.dt.float32r
ALU = mybir.AluOpType
ACT = mybir.ActivationFunctionType

P = 128
D = 2048
KT = D // P
T = 256
NT = 2 * T // P
NH = 8
LIN = 1024
CONV_K = 5
D_FF = 4 * D
FT = D_FF // P
EPS = 1e-6
GRID_W = 64
POOL_SIZES = (2, 4, 8, 16)
DECAY_START = 4 * LIN
POOL_START = DECAY_START + 32
IN_COLS = POOL_START + LIN
NB = 4
BK = KT // NB
UNIT = 2048
HALF = UNIT // 2
MOD_AT = 1
NRAW = 4
NHL = 4
CH = P
NCH = NT
NCHAIN = 2 * NH
LEVELS = 6

K_UNITS = [(LIN, 1), (LIN + 512, 1)]
V_UNITS = [(2 * LIN, 1), (2 * LIN + 512, 1)]
Q_UNITS = [(0, 0), (512, 0)]
Z_UNITS = [(3 * LIN, 0), (3 * LIN + 512, 0)]
P_UNITS = [(POOL_START, 0), (POOL_START + 512, 0)]
IN_UNITS = K_UNITS + V_UNITS + Q_UNITS + Z_UNITS + P_UNITS
NU = len(IN_UNITS)
HB = 2 * NU
N_IN = NB * NU
N_OUT = 16
N_UP = 64
N_DOWN = 64


IN_ORDER = [[0, 4, 1, 5, 2, 6, 3, 7, 8, 9]] * (NB - 1) + [list(range(NU))]


def unit_of(m):
    return IN_ORDER[m // HB][m % HB // 2]


def bank_plan():
    plan, n = [], 0
    for m in range(NB * HB):
        plan.append(list(range(n, n + (2 if IN_UNITS[unit_of(m)][1] else 1))))
        n += len(plan[-1])
    return plan


def last_banks(m):
    b = m // HB - 1
    return PLAN[HB * b + 2 * IN_ORDER[b].index(unit_of(m)) + m % 2]


PLAN = bank_plan()


def build(nc, x, c, ctx_in, c_ctx, w_ada, b_ada, norm1_w, norm2_w, w_in, conv_w, a_log, dt_bias,
          onorm_w, pool_w, pool_scale, w_out, w_up, w_down, final_norm_w, out):
    est = ExitStack()
    with est:
        base = (nc.sbuf_base + 63) // 32 * 32
        limit = nc.sbuf_usable_end
        est.enter_context(nc.allow_non_contiguous_dma(reason="small vectors"))

        def at(name, shape, off, dt=F32):
            size = 4
            for s in shape[1:]:
                size *= s
            assert base + off + size <= limit, (name, off + size, limit - base)
            return nc.alloc_sbuf_tensor_at(name, shape, dt, offset=base + off)

        def sem(name):
            return est.enter_context(nc.semaphore(name))

        KB = 1024
        raw = at("raw", [P, NRAW, UNIT], 0)
        w_hi = at("w_hi", [P, NHL, HALF], 32 * KB, F32R)
        w_lo = at("w_lo", [P, NHL, HALF], 48 * KB, F32R)
        ada = at("ada", [P, 2, UNIT], 64 * KB)
        C0 = 80 * KB
        ident = at("ident", [P, P], C0)
        ones = at("ones", [P, P], C0 + 512)
        col_a = at("col_a", [P, 8, KT], C0 + 1024)
        col_b = at("col_b", [P, P], C0 + 1536)
        cond = at("cond", [P, KT, 2], C0 + 2048)
        scale1 = at("scale1", [P, KT, 2], C0 + 2176)
        shift1 = at("shift1", [P, KT, 2], C0 + 2304)
        scale2 = at("scale2", [P, KT], C0 + 2432)
        shift2 = at("shift2", [P, KT], C0 + 2496)
        ssq = at("ssq", [P, 4], C0 + 2560)
        rms = at("rms", [P, 4], C0 + 2592)
        onorm = at("onorm", [P, 1], C0 + 2624)
        eps_c = at("eps_c", [P, 1], C0 + 2656)
        one_c = at("one_c", [P, 1], C0 + 2688)
        dtb = at("dtb", [P, 16], C0 + 2720)
        alog = at("alog", [P, 16], C0 + 2784)
        gcum = at("gcum", [P, NT, 16], C0 + 2848)
        beta = at("beta", [P, NT, 16], C0 + 3104)
        nbeta = at("nbeta", [P, NT, 16], C0 + 3360)
        neg_eg = at("neg_eg", [P, NT, 16], C0 + 3616)
        e_tail = at("e_tail", [P, NT, 16], C0 + 3872)
        e_last = at("e_last", [P, NT, 16], C0 + 4128)
        R0 = C0 + 4384
        m_low = at("m_low", [P, LEVELS + 1, P], R0)
        m_up = at("m_up", [P, LEVELS + 1, P], R0 + 3584)
        mod_acc = at("mod_acc", [P, 4, 512], R0 - 1024)
        A0 = R0 + 7168
        acc_kv = at("acc_kv", [P, 16, 2 * T], A0)
        acc_x = at("acc_x", [P, 24, T], A0 + 32 * KB)
        F0 = A0 + 56 * KB
        xT = at("xT", [P, KT, 2 * T], F0)
        xn_hi = at("xn_hi", [P, BK, 2 * T], F0 + 32 * KB, F32R)
        xn_lo = at("xn_lo", [P, BK, 2 * T], F0 + 40 * KB, F32R)
        wab_hi = at("wab_hi", [P, KT, 32], F0 + 48 * KB, F32R)
        wab_lo = at("wab_lo", [P, KT, 32], F0 + 50 * KB, F32R)
        mod0 = at("mod0", [P, 8, UNIT], 16 * KB)
        x_nat = at("x_nat", [P, NT, D], A0)
        wab_raw = at("wab_raw", [P, KT, 32], A0 + 32 * KB)
        rows_a = at("rows_a", [P, P], A0 + 34 * KB)
        rows_b = at("rows_b", [P, P], A0 + 34 * KB + 512)
        row_tile = at("row_tile", [P, 2, HALF], 0)
        row_acc = at("row_acc", [P, 2, UNIT], 8 * KB)
        XT = at("XT", [P, NCHAIN, 512], F0)
        At = at("At", [P, NCHAIN, T], F0 + 32 * KB)
        KK = at("KK", [P, 2, 512], F0 + 48 * KB)
        QK = at("QK", [P, 2, T], F0 + 52 * KB)
        gcT = at("gcT", [16, 512], F0 + 54 * KB)
        Eb = at("Eb", [P, 2, 512], F0 + 56 * KB)
        Xb = at("Xb", [P, 2, 4, 512], 32 * KB)
        MT = at("MT", [P, 2, 4, 512], 48 * KB)
        sel = at("sel", [16, 16, P], 64 * KB)
        Mn = at("Mn", [P, 512], 72 * KB)
        Pb = at("Pb", [P, 2, 512], 74 * KB)
        tri = at("tri", [P, 4, P], 78 * KB)
        UI, LI, SU, SL = range(4)
        l2b = at("l2b", [P, 12, 512], F0)
        cbuf = at("cbuf", [P, 4, 512], F0 + 24 * KB)
        g_in = at("g_in", [P, NT, 16], 46 * KB)
        g_t1 = at("g_t1", [P, NT, 16], 46 * KB + 256)
        g_t2 = at("g_t2", [P, NT, 16], 46 * KB + 512)
        g_log = at("g_log", [P, NT, 16], 46 * KB + 768)
        k_nat = at("k_nat", [P, NH, NCH, P], 32 * KB)
        qd_b = at("qd_b", [P, NH, T], 48 * KB)
        rb = at("rb", [P, 4, 512], 56 * KB)
        vn = at("vn", [P, 4, 512], 64 * KB)
        vt = at("vt", [P, 4, 512], 72 * KB)
        Sb = at("Sb", [P, NCHAIN, P], F0 + 48 * KB)
        eg_row = at("eg_row", [P, 2, T], F0 + 56 * KB)
        pp = at("pp", [P, 2, 8, 80], 24 * KB)
        icol = at("icol", [P, 4, GRID_W], 24 * KB + 5120)
        inv = at("inv", [P, 4, GRID_W], 24 * KB + 6144)
        o_sb = at("o_sb", [P, NH, T], 32 * KB)
        o_sq = at("o_sq", [P, NH, T], 40 * KB)
        o_rs = at("o_rs", [P, NH, T], 48 * KB)
        mixT = at("mixT", [P, KT, T], A0)
        mix_hi = at("mix_hi", [P, KT, T], F0, F32R)
        mix_lo = at("mix_lo", [P, KT, T], F0 + 16 * KB, F32R)
        g1_acc = at("g1_acc", [P, UNIT], 0)
        g1_tile = at("g1_tile", [P, 4, HALF], 8 * KB)
        gate1 = at("gate1", [P, D], F0 + 40 * KB)
        yt = at("yt", [P, 2, 512], F0 + 48 * KB)
        x2 = at("x2", [P, 2, D], R0 + 24 * KB + 64 * KB + 32 * KB - 120 * KB)
        g2_acc = at("g2_acc", [P, UNIT], R0 + 16 * KB)
        xn2_hi = at("xn2_hi", [P, KT, T], R0 + 24 * KB, F32R)
        xn2_lo = at("xn2_lo", [P, KT, T], R0 + 40 * KB, F32R)
        hT = at("hT", [P, FT, T], R0 + 56 * KB)
        xs2 = at("xs2", [P, 2, D], R0 + 56 * KB)
        xT2 = at("xT2", [P, KT, T], R0 + 72 * KB)
        sq2 = at("sq2", [P, 2, D], R0 + 88 * KB)
        gate2 = at("gate2", [P, D], R0 + 24 * KB)
        fin_w = at("fin_w", [P, D], R0 + 32 * KB)
        h_hi = at("h_hi", [P, 4, T], R0 + 40 * KB, F32R)
        h_lo = at("h_lo", [P, 4, T], R0 + 44 * KB, F32R)
        zero_r = at("zero_r", [P, 512], R0 + 48 * KB, F32R)
        yt2 = at("yt2", [P, 2, 512], R0 + 50 * KB)

        ps = est.enter_context(nc.psum_tensor("ps", [P, 8, 512], F32))

        S = {}

        def s(name):
            if name not in S:
                S[name] = sem(name)
            return S[name]

        raw_in = [sem(f"raw_in{i}") for i in range(NRAW)]
        mod0_in = [sem(f"mod0_in{i}") for i in range(8)]
        gate_in = [sem(f"gate_in{i}") for i in range(2)]
        row_in = [sem(f"row_in{i}") for i in range(2)]
        g1_in = [sem(f"g1_in{i}") for i in range(4)]
        mod_in = [sem(f"mod_in{i}") for i in range(2)]
        x_in = [sem(f"x_in{i}") for i in range(NT)]
        block = est.enter_context(nc.Block())
        w_ada0, w_in0, w_out0, w_up0, w_down0 = w_ada[0], w_in[0], w_out[0], w_up[0], w_down[0]

        def unit_src(n):
            if n < N_IN:
                b, c0 = n // NU, IN_UNITS[unit_of(2 * n)][0]
                return w_in0[b * 512:(b + 1) * 512, c0:c0 + 512].rearrange("(k p) c -> p k c", p=P)
            if n < N_IN + N_OUT:
                m = n - N_IN
                ch, k2 = m // 8, m % 8
                return w_out0[k2 * 256:(k2 + 1) * 256, ch * 1024:(ch + 1) * 1024].rearrange("(k p) c -> p k c", p=P)
            raise AssertionError

        def unit_dst(slot, form):
            k = 4 if form == 4 else 2
            return raw[:, slot, :].rearrange("p (k c) -> p k c", k=k)

        def load_unit(eng, n):
            if n >= NRAW:
                wait_lo(eng, 2 * (n - NRAW) + 1)
            eng.dma_start(unit_dst(n % NRAW, 4 if n < N_IN else 2), unit_src(n)).then_inc(raw_in[n % NRAW], 16)

        def raw_half(n2, strided):
            slot, hb = (n2 // 2) % NRAW, n2 % 2
            if strided:
                return raw[:, slot, :].rearrange("p (k c) -> p k c", k=4)[:, :, hb * 256:(hb + 1) * 256]
            return raw[:, slot, hb * HALF:(hb + 1) * HALF]

        def part_slot(t, n2, strided):
            v = t[:, n2 % NHL, :]
            return v.rearrange("p (k c) -> p k c", k=4) if strided else v

        def hi_split(eng, n2):
            strided = n2 < 2 * N_IN
            if n2 % 2 == 0:
                eng.wait_ge(raw_in[(n2 // 2) % NRAW], 16 * (n2 // 2 // NRAW + 1))
            if n2 >= NHL:
                wait_used(eng, n2 - NHL)
            eng.activation(part_slot(w_hi, n2, strided), raw_half(n2, strided), ACT.Copy).then_inc(s("hi_done"), 1)

        def on_pool(n2):
            return n2 < 2 * N_IN and not IN_UNITS[unit_of(n2)][1]

        def wait_lo(eng, n2):
            count = sum(on_pool(i) == on_pool(n2) for i in range(n2 + 1))
            eng.wait_ge(s("lo_pool" if on_pool(n2) else "lo_done"), count)

        LO = sum(not on_pool(i) for i in range(2 * N_IN)) - 2 * N_IN

        def lo_split(eng, n2):
            strided = n2 < 2 * N_IN
            eng.wait_ge(s("hi_done"), n2 + 1)
            eng.tensor_tensor(part_slot(w_lo, n2, strided), raw_half(n2, strided),
                              part_slot(w_hi, n2, strided).bitcast(F32), ALU.subtract
                              ).then_inc(s("lo_pool" if on_pool(n2) else "lo_done"), 1)

        def load_mod(eng, j):
            part, g = j // 4, j % 4
            src = w_ada0[g * 512:(g + 1) * 512, part * D:part * D + 512]
            eng.dma_start(mod0[:, j, :].rearrange("p (k c) -> p k c", k=4),
                          src.rearrange("(k p) c -> p k c", p=P)).then_inc(mod0_in[j], 16)

        def load_row_half(eng, n):
            if n >= 2:
                eng.wait_ge(s("row_sum"), n - 1)
            part, kk, cc = 3 + n // 32, n // 2 % 16, n % 2
            eng.dma_start(row_tile[:, cc, :],
                          w_ada0[kk * P:(kk + 1) * P, part * D + cc * HALF:part * D + (cc + 1) * HALF]
                          ).then_inc(row_in[cc], 16)

        STEPS = 26

        def row_halves_at(step):
            return [n for n in range(64) if STEPS + n * 6 // 5 == step]

        def load_mod_half(eng, b, h):
            if b == 1 and h < 2:
                eng.wait_ge(s("ada_pe"), 8)
            else:
                eng.wait_ge(s("mod_half"), 2 * (16 * (b - 1) + h - 1))
            part, g = h // 8, h % 8
            src = w_ada0[g * 256:(g + 1) * 256, part * D + b * 512:part * D + (b + 1) * 512]
            eng.dma_start(ada[:, 1, (h % 2) * HALF:(h % 2 + 1) * HALF].rearrange("p (k c) -> p k c", k=2),
                          src.rearrange("(k p) c -> p k c", p=P)).then_inc(mod_in[h % 2], 16)

        def wait_used(eng, n2):
            if n2 < 2 * N_IN:
                eng.wait_ge(s("pj"), PLAN[n2][-1] + 1)
            else:
                eng.wait_ge(s("w_used"), n2 - 2 * N_IN + 1)

        N_MASKS = 2 + (LEVELS + 1) * 6 + 2 + 5
        N0 = PLAN[HB - 1][-1] + 1
        PJ_DVE = PLAN[-1][-1] + 1 - N0

        def tap(i, k):
            tile = (i + 8) if i < 16 else i - 16
            return col_b[:, k * 24 + tile:k * 24 + tile + 1]

        def gb_bank(r):
            return 6 + r % 2

        def t1_bank(r):
            return 7 - r % 2

        def t2_bank(r):
            return 6 + r % 2

        def inverted(r):
            return 24 * (r // 4) + 20 + r % 4 + 1

        def chunk_at(st, d):
            return ((2, 3, 0, 1), (3, 2, 1, 0))[d][st]

        def bc(ap, n):
            return ap.unsqueeze(1).to_broadcast([P, n, ap.shape[-1]])

        def bc_in(ap, n):
            return ap.unsqueeze(2).to_broadcast([P, ap.shape[-1], n])

        def acc_of(u, hb, i, both):
            if both:
                return acc_kv[:, 4 * u + 2 * hb + i, :]
            t = 4 * (u - 4) + 2 * hb
            return acc_x[:, t:t + 2, :].rearrange("p a c -> p (a c)")

        @block.sync
        def _(sp):
            sp.wait_ge(s("rows_in"), 160)
            for t in range(NT):
                src = (x if t < 2 else ctx_in)[0][(t % 2) * P:(t % 2 + 1) * P, :]
                sp.dma_start(x_nat[:, t, :], src).then_inc(x_in[t], 16)
            for j in range(8):
                load_mod(sp, j)
            for n in range(NRAW):
                if n == 2:
                    sp.wait_ge(s("ada_pe"), 2)
                load_unit(sp, n)
            for b in range(NB):
                for u in range(NU):
                    if NU * b + u + NRAW < N_IN:
                        load_unit(sp, NU * b + u + NRAW)
            wait_lo(sp, 2 * N_IN - 3)
            wait_lo(sp, 2 * N_IN - 1)
            for n in range(64):
                load_row_half(sp, n)
            sp.wait_ge(s("g1_z"), 1)
            sp.dma_start(g1_acc[0:1, :], b_ada[0:1, 2 * D:3 * D]).then_inc(s("g1_b"), 16)
            sp.wait_ge(s("red_mm"), 1)
            for n in range(2 * KT):
                kk, cc = n // 2, n % 2
                if n >= 4:
                    sp.wait_ge(s("g1_pool" if cc else "ada_dve"), n // 2 - 1)
                sp.dma_start(g1_tile[:, n % 4, :],
                             w_ada0[kk * P:(kk + 1) * P, 2 * D + cc * HALF:2 * D + (cc + 1) * HALF]
                             ).then_inc(g1_in[n % 4], 16)
            sp.wait_ge(s("o_mm"), 1)
            sp.dma_start(ada[:, 1, :].rearrange("p (k c) -> p k c", k=8),
                         pool_w[0].rearrange("g (i p) o -> p (g i) o", p=P)).then_inc(s("pool_w_in"), 16)
            sp.wait_ge(s("g1_mm"), 4)
            sp.wait_ge(s("pool_d"), 4)
            for n in range(N_IN, N_IN + NRAW):
                load_unit(sp, n)
            for n in range(N_IN + NRAW, N_IN + N_OUT):
                load_unit(sp, n)
                if n == N_IN + NRAW + 1:
                    sp.wait_ge(s("mixl"), KT)
                    sp.dma_start(x2[:, :, :], x[0].rearrange("(t p) d -> p t d", p=P)).then_inc(s("xres_in"), 16)
            U0 = N_IN + N_OUT

            def up_unit(it, k):
                sp.wait_ge(s("lo_done"), it * 16 + LO + 2 * (U0 + k - NRAW) + 2)
                sp.dma_start(unit_dst(k % NRAW, 4),
                             w_up0[(k % 4) * 512:(k % 4 + 1) * 512, ds(it * 1024 + (k // 4) * 512, 512)]
                             .rearrange("(k p) c -> p k c", p=P)).then_inc(raw_in[k % NRAW], 16)

            def gate_unit(it, j):
                sp.wait_ge(s("ada_dve"), it * 2 + KT + j - 1)
                sp.dma_start(ada[:, j, :], w_ada0[ds(it * (2 * P) + j * P, P), 5 * D:6 * D]).then_inc(gate_in[j], 16)

            sp.wait_ge(s("g2_z"), 1)
            sp.dma_start(g2_acc[0:1, :], b_ada[0:1, 5 * D:6 * D]).then_inc(s("g2_b"), 16)
            with sp.Fori(0, 8) as it:
                for k in range(8):
                    up_unit(it, k)
                    if k in (2, 6):
                        gate_unit(it, k // 4)
            D0 = U0 + N_UP
            sp.wait_ge(s("w_used"), 2 * (N_OUT + N_UP))
            sp.dma_start(fin_w[:, :], final_norm_w.partition_broadcast(P)).then_inc(s("fin_in"), 16)
            for ch in range(2):
                with sp.Fori(0, 8) as it:
                    for k in range(4):
                        sp.wait_ge(s("lo_done"), it * 8 + LO + 2 * (D0 + 32 * ch + k - NRAW) + 2)
                        sp.dma_start(unit_dst(k % NRAW, 2),
                                     w_down0[ds(it * 1024 + k * 256, 256), ch * 1024:(ch + 1) * 1024]
                                     .rearrange("(k p) c -> p k c", p=P)).then_inc(raw_in[k % NRAW], 16)
            for t in range(2):
                sp.wait_ge(s("fin_c"), t + 1)
                sp.dma_start(out[0][t * P:(t + 1) * P, :], x2[:, t, :]).then_inc(s("stored"), 16)
            sp.wait_ge(s("stored"), 32)

        @block.gpsimd
        def _(pool):
            pool.memset(ones[:, :], 1.0).then_inc(s("const_z"), 1)
            pool.memset(ident[:, :], 0.0).then_inc(s("const_z"), 1)
            pool.memset(eps_c[:, :], EPS).then_inc(s("const_z"), 1)
            pool.memset(one_c[:, :], 1.0).then_inc(s("const_z"), 1)
            pool.wait_ge(s("const_z"), 4)
            pool.affine_select(out=ident[:, :], in_=ident[:, :], compare_op=ALU.not_equal, fill=1.0, base=0,
                               pattern=[[-1, P]], channel_multiplier=1).then_inc(s("const_done"), 1)
            def level_masks():
                pool.wait_ge(s("ada_pe"), 8 + NB - 1)
                pool.memset(m_low[:, :, :], 0.0).then_inc(s("masks"), 1)
                pool.memset(m_up[:, :, :], 0.0).then_inc(s("masks"), 1)
                pool.wait_ge(s("masks"), 2)
                n = 2
                for lv in range(LEVELS + 1):
                    hw, nb = 1 << lv, P >> (lv + 1)
                    lo_v = m_low[:, lv, :].rearrange("p (b t j) -> p b t j", t=2, j=hw)
                    up_v = m_up[:, lv, :].rearrange("p (b t j) -> p b t j", t=2, j=hw)
                    pool.memset(lo_v[:, :, 0, :], 1.0).then_inc(s("masks"), 1)
                    pool.memset(up_v[:, :, 1, :], 1.0).then_inc(s("masks"), 1)
                    n += 2
                    pool.wait_ge(s("masks"), n)
                    for v, base_ge, base_le in ((m_low, -hw, 2 * hw - 1), (m_up, 0, hw - 1)):
                        w = v[:, lv, :].rearrange("p (b j) -> p b j", j=2 * hw)
                        pool.affine_select(out=w, in_=w, compare_op=ALU.is_ge, fill=0.0, base=base_ge,
                                           pattern=[[-2 * hw, nb], [0, 2 * hw]], channel_multiplier=1
                                           ).then_inc(s("masks"), 1)
                        n += 1
                        pool.wait_ge(s("masks"), n)
                        pool.affine_select(out=w, in_=w, compare_op=ALU.is_ge, fill=0.0, base=base_le,
                                           pattern=[[2 * hw, nb], [0, 2 * hw]], channel_multiplier=-1
                                           ).then_inc(s("masks"), 1)
                        n += 1
                pool.wait_ge(s("mod_half"), 2 * 16 * (NB - 1))
                pool.memset(tri[:, :, :], 1.0).then_inc(s("masks"), 1)
                pool.memset(sel[:, :, :], 0.0).then_inc(s("masks"), 1)
                n += 2
                pool.wait_ge(s("masks"), n)
                for i, (sgn, b0) in enumerate([(1, 0), (-1, 0), (1, -1), (-1, -1)]):
                    pool.affine_select(out=tri[:, i, :], in_=tri[:, i, :], compare_op=ALU.is_ge, fill=0.0, base=b0,
                                       pattern=[[sgn, P]], channel_multiplier=-sgn).then_inc(s("masks"), 1)
                    n += 1
                pool.affine_select(out=sel[:, :, :], in_=sel[:, :, :], compare_op=ALU.not_equal, fill=1.0, base=0,
                                   pattern=[[-1, 16], [0, P]], channel_multiplier=1).then_inc(s("masks"), 1)
                n += 1
                assert n == N_MASKS, n

            pool.wait_ge(s("ada_pe"), 6)
            for n2 in range(2 * N_IN):
                if n2 == (NB - 1) * HB:
                    level_masks()
                if on_pool(n2):
                    lo_split(pool, n2)
            def decayed(r):
                h, d = r // 2, r % 2
                pool.wait_ge(s("kk_ev"), 4 * (h + 1))
                pool.wait_ge(s("e_exp"), r + 1)
                pool.tensor_tensor(At[:, r, :], QK[:, d, :], Eb[:, r % 2, 0:T], ALU.mult).then_inc(s("at_pool"), 1)
                pool.wait_ge(s("at_pool"), r + 1)
                pool.tensor_tensor(Eb[:, r % 2, :], KK[:, d, :], Eb[:, r % 2, :], ALU.mult).then_inc(s("am_pool"), 1)

            def sum_row_half(n):
                o = row_acc[:, n // 32, (n % 2) * HALF:(n % 2 + 1) * HALF]
                pool.wait_ge(s("row_scaled"), n + 1)
                pool.wait_ge(s("row_sum"), n)
                pool.tensor_tensor(o, o, row_tile[:, n % 2, :], ALU.add).then_inc(s("row_sum"), 1)

            for step_ in range(4 * STEPS):
                if step_ % STEPS % 6 == 2 and step_ % STEPS < 24:
                    decayed(4 * (step_ // STEPS) + step_ % STEPS // 6)
                for n in row_halves_at(step_):
                    if n % 32 >= 2:
                        sum_row_half(n)
            pool.wait_ge(s("row_sum"), 64)
            pool.memset(g1_acc[:, :], 0.0).then_inc(s("g1_z"), 1)
            n = 0

            def step(ins):
                nonlocal n
                n += 1
                ins.then_inc(s("pcnt"), 1)
                pool.wait_ge(s("pcnt"), n)

            step(pool.memset(pp[:, :, :, :], 0.0))
            HWP = 8
            for g, size in enumerate(POOL_SIZES):
                def count(i, nn):
                    return min(i + size - 1 - size // 2, nn - 1) - max(i - size // 2, 0) + 1
                counts = [count(i, GRID_W) for i in range(GRID_W)]
                step(pool.memset(icol[:, g, :], 1.0 / size))
                i = 0
                while i < GRID_W:
                    if counts[i] != size:
                        step(pool.memset(icol[:, g, i:i + 1], 1.0 / counts[i]))
                    i += 1
                for rr in range(4):
                    step(pool.tensor_scalar(inv[:, rr, :], icol[:, g, :], 1.0 / count(rr, 4), None, ALU.mult))
                u = acc_x[:, 16 + 2 * g:18 + 2 * g, :].rearrange("p a (r c) -> p (a r) c", c=GRID_W)
                cur = 0
                step(pool.tensor_copy(pp[:, 0, :, HWP:HWP + GRID_W], u))
                if g:
                    step(pool.memset(pp[:, 0, :, 0:HWP], 0.0))
                    step(pool.memset(pp[:, 0, :, HWP + GRID_W:], 0.0))
                w = 1
                while w < size:
                    lo_s, hi_s = (1, 0) if w == 1 else (w // 2, w // 2)
                    a, bnd = lo_s, 80 - hi_s
                    src, dst = pp[:, cur], pp[:, 1 - cur]
                    if a:
                        step(pool.memset(dst[:, :, 0:a], 0.0))
                    if bnd < 80:
                        step(pool.memset(dst[:, :, bnd:80], 0.0))
                    step(pool.tensor_tensor(dst[:, :, a:bnd], src[:, :, a - lo_s:bnd - lo_s],
                                            src[:, :, a + hi_s:bnd + hi_s], ALU.add))
                    cur, w = 1 - cur, 2 * w
                src = pp[:, cur, :, HWP:HWP + GRID_W].rearrange("p (a r) c -> p a r c", r=4)
                dst = pp[:, 1 - cur, :, HWP:HWP + GRID_W].rearrange("p (a r) c -> p a r c", r=4)
                lo_w, hi_w = size // 2, size - 1 - size // 2
                for rr in range(4):
                    lo_r, hi_r = max(rr - lo_w, 0), min(rr + hi_w, 3)
                    step(pool.tensor_copy(dst[:, :, rr, :], src[:, :, lo_r, :]))
                    for r2 in range(lo_r + 1, hi_r + 1):
                        step(pool.tensor_tensor(dst[:, :, rr, :], dst[:, :, rr, :], src[:, :, r2, :], ALU.add))
                for a_ in range(2):
                    step(pool.tensor_tensor(dst[:, a_], dst[:, a_], inv[:, :, :], ALU.mult))
                pool.tensor_tensor(u, pp[:, 1 - cur, :, HWP:HWP + GRID_W], u, ALU.subtract).then_inc(s("pool_d"), 1)
                pool.wait_ge(s("pool_d"), g + 1)
            for kk in range(KT):
                if kk == 0:
                    pool.wait_ge(s("g1_b"), 16)
                else:
                    pool.wait_ge(s("g1_pool"), kk)
                pool.wait_ge(s("g1_scaled"), kk + 1)
                pool.tensor_tensor(g1_acc[:, HALF:], g1_acc[:, HALF:], g1_tile[:, (2 * kk + 1) % 4, :], ALU.add
                                   ).then_inc(s("g1_pool"), 1)
            pool.wait_ge(s("mixl"), KT)
            pool.memset(g2_acc[:, :], 0.0).then_inc(s("g2_z"), 1)
            pool.wait_ge(s("w_used"), 2 * (N_OUT + N_UP))
            pool.memset(zero_r[:, :].bitcast(F32), 0.0).then_inc(s("zr"), 1)

        @block.scalar
        def _(act):
            sm = s("rows_in")
            vecs = [c, c_ctx.rearrange("(a d) -> a d", a=1), norm1_w, norm2_w] + \
                   [b_ada[0:1, p * D:(p + 1) * D] for p in (0, 1, 3, 4)]
            for i, v in enumerate(vecs):
                act.dma_start(rows_a[KT * i:KT * (i + 1), :], v[0].rearrange("(k p) -> k p", p=P)).then_inc(sm, 16)
            act.dma_start(rows_b[0:120, :], conv_w[0].rearrange("k (j p) -> (k j) p", p=P)).then_inc(sm, 16)
            act.dma_start(rows_b[120:128, :], pool_scale[0].rearrange("(j p) -> j p", p=P)).then_inc(sm, 16)
            sm = s("small_in")
            act.dma_start(wab_raw[:, :, :],
                          w_in0[:, DECAY_START:POOL_START].rearrange("(k p) c -> p k c", p=P)).then_inc(sm, 16)
            act.dma_start(dtb[:, :], dt_bias[0].rearrange("a b -> (a b)").partition_broadcast(P)).then_inc(sm, 16)
            act.dma_start(alog[:, :], a_log[0].rearrange("a b -> (a b)").partition_broadcast(P)).then_inc(sm, 16)
            act.dma_start(onorm[:, :], onorm_w[0].rearrange("(p o) -> p o", o=1)).then_inc(sm, 16)
            act.wait_ge(s("cols_dve"), 1)
            act.activation(cond[:, :, :], col_a[:, 0:2, :].rearrange("p j k -> p k j"), ACT.Silu
                           ).then_inc(s("cond_done"), 1)
            for t in range(NT):
                act.wait_ge(x_in[t], 16)
                if t:
                    act.wait_ge(s("sq_done"), t)
                act.activation(xT[:, 0:4, :].rearrange("p k c -> p (k c)"), x_nat[:, t, :], ACT.Square,
                               accum_out=ssq[:, t:t + 1]).then_inc(s("sq_done"), 1)
            act.wait_ge(s("sq_done"), NT)
            act.wait_ge(s("const_z"), 4)
            act.activation(rms[:, :], ssq[:, :], ACT.Ln, bias=eps_c[:, :], scale=1.0 / D).then_inc(s("ms"), 1)
            act.wait_ge(s("ms"), 1)
            act.activation(rms[:, :], rms[:, :], ACT.Exp, scale=-0.5).then_inc(s("rms_done"), 1)
            act.wait_ge(s("small_in"), 64)
            act.activation(wab_hi[:, :, :], wab_raw[:, :, :], ACT.Copy).then_inc(s("wab_h"), 1)
            for kt in range(0, KT, 2):
                act.wait_ge(s("xt_mm"), kt + 1)
                act.copy(xT[:, kt, :], ps[:, kt % 4, :]).then_inc(s("xt_act"), 1)
            act.wait_ge(s("ada_pe"), 4)
            for n2 in range(3):
                hi_split(act, n2)

            def conv_in(i):
                return acc_kv[:, i, :] if i < 16 else acc_x[:, i - 16, :]

            def centre(i):
                n = 512 if i < 16 else 256
                banks = PLAN[(NB - 1) * HB + i // 2]
                act.wait_ge(s("pj_dve"), banks[i % 2 if i < 16 else 0] - N0 + 1)
                if i >= 4:
                    act.wait_ge(s("silu"), i - 3)
                act.activation(cbuf[:, i % 4, 0:n], conv_in(i), ACT.Copy, scale=tap(i, 2)).then_inc(s("conv0"), 1)

            def finish(i):
                n = 512 if i < 16 else 256
                act.wait_ge(s("conv"), 4 * (i + 1))
                act.activation(conv_in(i), cbuf[:, i % 4, 0:n], ACT.Silu).then_inc(s("silu"), 1)
                if i < 8:
                    act.wait_ge(s("silu"), i + 1)
                    act.activation(l2b[:, i, :], acc_kv[:, i, :], ACT.Square).then_inc(s("l2_sq"), 1)
                elif i >= 16 and i % 2:
                    j = 8 + (i - 16) // 2
                    act.wait_ge(s("silu"), i + 1)
                    act.activation(l2b[:, j, :], l2_src(j), ACT.Square).then_inc(s("l2_sq"), 1)

            def l2_src(j):
                return acc_kv[:, j, :] if j < 8 else acc_x[:, 2 * (j - 8):2 * (j - 8) + 2, :].rearrange("p a c -> p (a c)")

            def evac_in(m):
                u, hb = unit_of(m), m % 2
                both = IN_UNITS[u][1]
                for i, no in enumerate(PLAN[m]):
                    act.wait_ge(s("pj"), no + 1)
                    act.copy(acc_of(u, hb, i, both), ps[:, no % 4, :]).then_inc(s("pj_act"), 1)

            for b in range(NB):
                for m in range(HB):
                    n2 = HB * b + m
                    if n2 >= 3:
                        hi_split(act, n2)
                    if MOD_AT <= m < MOD_AT + 16 and b < NB - 1:
                        load_mod_half(act, b + 1, m - MOD_AT)
                    if 0 <= n2 - 3 < HB:
                        evac_in(n2 - 3)
                    if b == NB - 1 and 3 <= m < 17:
                        if m == 3:
                            act.wait_ge(s("xnl"), KT)
                        for i in (2 * (m - 5), 2 * (m - 5) + 1):
                            if i >= 0:
                                finish(i)
                        for i in (2 * (m - 3), 2 * (m - 3) + 1):
                            if i < 24:
                                centre(i)
                    if m == 2:
                        for kt in range(BK):
                            if b and kt == 0:
                                wait_used(act, HB * b - 1)
                            act.wait_ge(s("mod_done"), 4 * b + kt + 1)
                            act.copy(xn_hi[:, kt, :], xT[:, BK * b + kt, :]).then_inc(s("xnh"), 1)
            act.wait_ge(s("pj_dve"), PJ_DVE)
            act.activation(acc_x[:, 8:16, :], acc_x[:, 8:16, :], ACT.Silu).then_inc(s("zsilu"), 1)
            act.wait_ge(s("gp"), 3)
            act.activation(g_t2[:, :, :], g_t1[:, :, :], ACT.Exp).then_inc(s("gp_act"), 1)
            act.activation(beta[:, :, :], nbeta[:, :, :], ACT.Exp, scale=-1.0).then_inc(s("gp_act"), 1)
            act.wait_ge(s("gp_act"), 2)
            act.activation(alog[:, :], alog[:, :], ACT.Exp).then_inc(s("gp_act"), 1)
            act.activation(g_t2[:, :, :], g_t2[:, :, :], ACT.Ln, bias=one_c[:, :]).then_inc(s("gp_act"), 1)
            for j in range(12):
                act.wait_ge(s("l2_mm"), j + 1)
                act.activation(l2b[:, j, :], ps[:, j % 2, :], ACT.Ln, bias=eps_c[:, :]).then_inc(s("l2_ln"), 1)
            for j in range(3):
                act.wait_ge(s("l2_ln"), 12)
                act.activation(l2b[:, 4 * j:4 * j + 4, :], l2b[:, 4 * j:4 * j + 4, :], ACT.Exp, scale=-0.5
                               ).then_inc(s("l2_rs"), 1)
            act.wait_ge(s("gc_ev"), 3)
            act.activation(neg_eg[:, :, :], gcum[:, :, :], ACT.Exp).then_inc(s("gp_act"), 1)
            act.activation(e_tail[:, :, :], e_tail[:, :, :], ACT.Exp).then_inc(s("gp_act"), 1)
            act.activation(e_last[:, :, :], e_last[:, :, :], ACT.Exp).then_inc(s("gp_act"), 1)
            act.wait_ge(s("gcT_mm"), 1)
            act.copy(gcT[:, :], ps[0:16, 5, :]).then_inc(s("gcT_ev"), 1)
            def decay_exp(r):
                act.wait_ge(s("gb_ev"), 4 * (r + 1))
                act.activation(Eb[:, r % 2, :], Eb[:, r % 2, :], ACT.Exp).then_inc(s("e_exp"), 1)

            def mt_copy(r):
                act.wait_ge(s("t2_mm"), r + 1)
                if r >= 8:
                    act.wait_ge(s("x_upd"), inverted(r - 8 + 3 - r % 4))
                act.copy(MT[:, (r // 4) % 2, r % 4, :], ps[:, t2_bank(r), :]).then_inc(s("mt_ev"), 1)

            def row_half(n):
                act.wait_ge(row_in[n % 2], 16 * (n // 2 + 1))
                sc = cond[:, n // 2 % 16, 0:1]
                if n % 32 < 2:
                    o = row_acc[:, n // 32, (n % 2) * HALF:(n % 2 + 1) * HALF]
                    if n:
                        act.wait_ge(s("row_sum"), n)
                    act.activation(o, row_tile[:, n % 2, :], ACT.Copy, scale=sc).then_inc(s("row_sum"), 1)
                    act.wait_ge(s("row_sum"), n + 1)
                    act.sem_inc(s("row_scaled"), 1)
                else:
                    act.activation(row_tile[:, n % 2, :], row_tile[:, n % 2, :], ACT.Copy, scale=sc
                                   ).then_inc(s("row_scaled"), 1)

            for step_ in range(4 * STEPS):
                r, j = 4 * (step_ // STEPS) + step_ % STEPS // 6, step_ % STEPS % 6
                if step_ % STEPS < 24:
                    if j == 2:
                        decay_exp(r)
                    if j == 5:
                        mt_copy(r)
                for n in row_halves_at(step_):
                    row_half(n)
            for r in range(NCHAIN):
                act.wait_ge(s("er_mm"), r + 1)
                if r >= 2:
                    act.wait_ge(s("qd"), r - 1)
                act.activation(eg_row[:, r % 2, :], ps[:, r % 2, 0:T], ACT.Exp).then_inc(s("er_exp"), 1)
                if r < NH:
                    act.wait_ge(s("x_upd"), inverted(NCHAIN - 1))
                    act.wait_ge(s("ktr"), r + 1)
                    act.copy(k_nat[:, r].rearrange("p a b -> p (a b)"), ps[:, 2 + r % 2, :]).then_inc(s("kn_ev"), 1)
            def gate_scaled(kk):
                n = 2 * kk + 1
                act.wait_ge(g1_in[n % 4], 16 * (n // 4 + 1))
                act.activation(g1_tile[:, n % 4, :], g1_tile[:, n % 4, :], ACT.Copy, scale=cond[:, kk, 0:1]
                               ).then_inc(s("g1_scaled"), 1)

            for st in range(3):
                for g in range(4):
                    gate_scaled(4 * st + g)
                    act.wait_ge(s("vn_ev"), 4 * st + g + 1)
                    if st:
                        act.wait_ge(s("su_mm"), 4 * (st - 1) + g + 1)
                    for q in range(4):
                        h, d = 2 * g + q // 2, q % 2
                        t = chunk_at(st, d)
                        act.activation(vt[:, g, q * P:(q + 1) * P], vn[:, g, q * P:(q + 1) * P], ACT.Copy,
                                       scale=e_tail[:, t, 8 * d + h:8 * d + h + 1]).then_inc(s("vt_ev"), 1)
            for kk in range(12, KT):
                gate_scaled(kk)
            for i in range(4):
                act.wait_ge(s("g1_mm"), i + 1)
                act.copy(gate1[:, i * 512:(i + 1) * 512], ps[:, 2 + i % 2, :]).then_inc(s("g1_ev"), 1)
            act.wait_ge(s("o_ev"), 4)
            act.activation(o_sq[:, :, :], o_sb[:, :, :], ACT.Square).then_inc(s("o_sqd"), 1)
            for i in range(4):
                act.wait_ge(s("on_mm"), i + 1)
                dst = o_rs[:, 2 * i:2 * i + 2, :].rearrange("p a b -> p (a b)")
                act.activation(dst, ps[:, 4 + i, :], ACT.Ln, bias=eps_c[:, :], scale=1.0 / P).then_inc(s("on_rs"), 1)
            act.wait_ge(s("on_rs"), 4)
            act.activation(o_rs[:, :, :], o_rs[:, :, :], ACT.Exp, scale=-0.5).then_inc(s("on_rs"), 1)
            for i in range(8):
                act.wait_ge(s("pw_mm"), i + 1)
                act.activation(mixT[:, 8 + i, :], ps[:, i % 2, 0:T], ACT.Copy, scale=col_b[:, 120 + i:121 + i]
                               ).then_inc(s("mix_pool"), 1)
            for kt in range(KT):
                if kt < 8:
                    act.wait_ge(s("mix_lin"), 1)
                else:
                    act.wait_ge(s("mix_pool"), 8)
                act.copy(mix_hi[:, kt, :], mixT[:, kt, :]).then_inc(s("mixh"), 1)
            act.wait_ge(s("mix_lin"), 1)
            O2 = 2 * N_IN
            for n2 in range(O2, O2 + 2 * N_OUT):
                hi_split(act, n2)
            H0 = 2 * (N_IN + N_OUT)

            def mlp_hi(it, k, h0, per):
                n2 = h0 + k
                if k % 2 == 0:
                    act.wait_ge(raw_in[(n2 // 2) % NRAW], it * (8 * per // NRAW) + 16 * (n2 // 2 // NRAW + 1))
                act.wait_ge(s("w_used"), it * per + n2 - NHL + 1 - 2 * N_IN)
                act.activation(w_hi[:, n2 % NHL, :],
                               raw[:, (n2 // 2) % NRAW, (n2 % 2) * HALF:(n2 % 2 + 1) * HALF],
                               ACT.Copy).then_inc(s("hi_done"), 1)

            for k in range(3):
                mlp_hi(0, k, H0, 16)
            for t in range(2):
                act.wait_ge(s("x2_done"), 8)
                act.activation(sq2[:, t, :], x2[:, t, :], ACT.Square, accum_out=ssq[:, t:t + 1]
                               ).then_inc(s("sq2_done"), 1)
            act.wait_ge(s("sq2_done"), 2)
            act.activation(rms[:, 0:2], ssq[:, 0:2], ACT.Ln, bias=eps_c[:, :], scale=1.0 / D).then_inc(s("m2"), 1)
            act.wait_ge(s("m2"), 1)
            act.activation(rms[:, 0:2], rms[:, 0:2], ACT.Exp, scale=-0.5).then_inc(s("rms2"), 1)
            for kt in range(KT):
                act.wait_ge(s("mod2"), kt + 1)
                act.copy(xn2_hi[:, kt, :], xT2[:, kt, :]).then_inc(s("xn2h"), 1)
            def up_act(it, ahead):
                for k in range(16):
                    if k < ahead:
                        mlp_hi(it, k + 3, H0, 16)
                    if k % 8 == 7:
                        for i in range(2):
                            bank = 2 * (k // 8) + i
                            f0 = 2 * bank
                            act.wait_ge(s("w_used"), it * 16 + H0 - 2 * N_IN + k + 1)
                            act.activation(hT[:, ds(it * 8 + f0, 2), :].rearrange("p a b -> p (a b)"),
                                           ps[:, bank, :], ACT.Relu).then_inc(s("relu_a"), 1)

            act.wait_ge(s("xn2l"), KT)
            with act.Fori(0, 7) as it:
                up_act(it, 16)
            up_act(7, 13)
            for i in range(4):
                act.wait_ge(s("g2_mm"), i + 1)
                act.copy(gate2[:, i * 512:(i + 1) * 512], ps[:, 4 + i, :]).then_inc(s("g2_ev"), 1)
            E0 = H0 + 2 * N_UP
            act.wait_ge(s("relu_v"), 32)
            for ch in range(2):
                with act.Fori(0, 8) as it:
                    for k in range(8):
                        mlp_hi(it, k, E0 + 64 * ch, 8)
                        act.copy(h_hi[:, k % 4, :], hT[:, ds(it * 8 + k, 1), :].rearrange("p a b -> p (a b)")
                                 ).then_inc(s("hh"), 1)
            for t in range(2):
                act.wait_ge(s("fin_a"), 8)
                act.activation(sq2[:, t, :], x2[:, t, :], ACT.Square, accum_out=ssq[:, 2 + t:3 + t]
                               ).then_inc(s("sq2_done"), 1)
            act.wait_ge(s("sq2_done"), 4)
            act.activation(rms[:, 2:4], ssq[:, 2:4], ACT.Ln, bias=eps_c[:, :], scale=1.0 / D).then_inc(s("m2"), 1)
            act.wait_ge(s("m2"), 2)
            act.activation(rms[:, 2:4], rms[:, 2:4], ACT.Exp, scale=-0.5).then_inc(s("rms2"), 1)

        @block.vector
        def _(dve):
            steps = [0]

            def step(ins, wait=True):
                steps[0] += 1
                ins.then_inc(s("dve_step"), 1)
                dve.wait_ge(s("dve_step"), steps[0])

            dve.wait_ge(s("rowsT"), 1)
            step(dve.tensor_copy(col_a[:, :, :], ps[:, 6, 0:P].rearrange("p (a b) -> p a b", a=8)))
            step(dve.tensor_copy(col_b[:, :], ps[:, 6, P:2 * P]))
            dve.tensor_scalar(col_a[:, 5, :], col_a[:, 5, :], 1.0, None, ALU.add)
            dve.tensor_scalar(col_a[:, 7, :], col_a[:, 7, :], 1.0, None, ALU.add).then_inc(s("cols_dve"), 1)
            dve.wait_ge(s("rms_done"), 1)
            for t in range(NT):
                dve.tensor_scalar(x_nat[:, t, :], x_nat[:, t, :], rms[:, t:t + 1], None, ALU.mult
                                  ).then_inc(s("xs_done"), 1)
            dve.wait_ge(s("wab_h"), 1)
            dve.tensor_tensor(wab_lo[:, :, :], wab_raw[:, :, :], wab_hi[:, :, :].bitcast(F32), ALU.subtract
                              ).then_inc(s("wab_l"), 1)
            for kt in range(1, KT, 2):
                dve.wait_ge(s("xt_mm"), kt + 1)
                dve.tensor_copy(xT[:, kt, :], ps[:, kt % 4, :]).then_inc(s("xt_dve"), 1)

            def modulation(b):
                dve.wait_ge(s("ada_pe"), 8 + b)
                kb = slice(BK * b, BK * b + BK)
                sums = ps[:, 4, 0:16].rearrange("p (s k j) -> p s k j", s=2, j=2)
                step(dve.tensor_tensor(scale1[:, kb, :], sums[:, 1], bc_in(col_a[:, 5, kb], 2), ALU.add))
                dve.tensor_tensor(shift1[:, kb, :], sums[:, 0], bc_in(col_a[:, 4, kb], 2), ALU.add
                                  ).then_inc(s("modc_done"), 1)
                step(dve.tensor_tensor(scale1[:, kb, :], scale1[:, kb, :], bc_in(col_a[:, 2, kb], 2), ALU.mult))
                if b == 0:
                    dve.wait_ge(s("xt_act"), KT // 2)
                for kt in range(BK * b, BK * b + BK):
                    for j in range(2):
                        ins = dve.tensor_scalar(xT[:, kt, j * T:(j + 1) * T], xT[:, kt, j * T:(j + 1) * T],
                                                scale1[:, kt, j:j + 1], shift1[:, kt, j:j + 1], ALU.mult, ALU.add)
                    ins.then_inc(s("mod_done"), 1)

            def evac_in(m):
                u, hb = unit_of(m), m % 2
                both = IN_UNITS[u][1]
                for i, no in enumerate(PLAN[m]):
                    dve.wait_ge(s("pj"), no + 1)
                    if m < 2 * HB:
                        dve.wait_ge(s("pj_act"), N0)
                    else:
                        dve.wait_ge(s("pj_dve"), last_banks(m)[i] - N0 + 1)
                    a = acc_of(u, hb, i, both)
                    dve.tensor_tensor(a, a, ps[:, no % 4, :], ALU.add).then_inc(s("pj_dve"), 1)

            def mod_half(b, h):
                part, g = h // 8, h % 8
                dve.wait_ge(mod_in[h % 2], 16 * (8 * (b - 1) + h // 2 + 1))
                if h == 0 and b > 1:
                    dve.wait_ge(s("ada_pe"), 8 + b - 1)
                for kk in range(2):
                    src = ada[:, 1, h % 2 * HALF + kk * 512:h % 2 * HALF + (kk + 1) * 512]
                    for j in range(2):
                        o, sc = mod_acc[:, 2 * part + j, :], cond[:, 2 * g + kk, j:j + 1]
                        if g == 0 and kk == 0:
                            ins = dve.tensor_scalar(o, src, sc, None, ALU.mult)
                        else:
                            if kk == 0:
                                dve.wait_ge(s("mod_half"), 2 * (16 * (b - 1) + h) - 2 + j + 1)
                            else:
                                dve.wait_ge(s("mod_first"), 2 * (16 * (b - 1) + h) + j + 1)
                            ins = dve.scalar_tensor_tensor(out=o, in0=src, scalar=sc, in1=o,
                                                           op0=ALU.mult, op1=ALU.add)
                        ins.then_inc(s("mod_half" if kk else "mod_first"), 1)

            def convolve(i):
                dve.wait_ge(s("conv0"), i + 1)
                for x_, k in enumerate((0, 1, 3, 4)):
                    d = k - CONV_K // 2
                    a, e = max(0, -d), T - max(0, d)
                    if i < 16:
                        u = acc_kv[:, i, :].rearrange("p (s t) -> p s t", s=2)
                        o = cbuf[:, i % 4, :].rearrange("p (s t) -> p s t", s=2)
                        u, o = u[:, :, a + d:e + d], o[:, :, a:e]
                    else:
                        u, o = acc_x[:, i - 16, a + d:e + d], cbuf[:, i % 4, a:e]
                    if x_:
                        dve.wait_ge(s("conv"), 4 * i + x_)
                    dve.scalar_tensor_tensor(out=o, in0=u, scalar=tap(i, k), in1=o, op0=ALU.mult, op1=ALU.add
                                             ).then_inc(s("conv"), 1)

            dve.wait_ge(s("cond_done"), 1)
            dve.wait_ge(s("ada_pe"), 6)
            for b in range(NB):
                for m in range(HB):
                    n2 = HB * b + m
                    if not on_pool(n2):
                        lo_split(dve, n2)
                    if n2 - 3 >= HB:
                        evac_in(n2 - 3)
                    if b == NB - 1 and 4 <= m < 16:
                        for i in (2 * (m - 4), 2 * (m - 4) + 1):
                            convolve(i)
                    if m == 2:
                        if b == 0:
                            modulation(0)
                        for kt in range(BK):
                            dve.wait_ge(s("xnh"), BK * b + kt + 1)
                            dve.tensor_tensor(xn_lo[:, kt, :], xT[:, BK * b + kt, :],
                                              xn_hi[:, kt, :].bitcast(F32), ALU.subtract).then_inc(s("xnl"), 1)
                    if 2 <= m < 18 and b < NB - 1:
                        mod_half(b + 1, m - 2)
                    if m == 19 and b < NB - 1:
                        modulation(b + 1)
            for m in range(NB * HB - 3, NB * HB):
                evac_in(m)
            dve.wait_ge(s("ab_done"), 1)
            dve.wait_ge(s("small_in"), 64)
            ab = ps[:, 5, 0:P].rearrange("p (t c) -> p t c", t=NT)
            wait_used(dve, 2 * N_IN - 1)
            dve.tensor_tensor(g_in[:, :, :], ab[:, :, 0:16], bc(dtb[:, :], NT), ALU.add).then_inc(s("gp"), 1)
            dve.tensor_copy(nbeta[:, :, :], ab[:, :, 16:32]).then_inc(s("gp"), 1)
            dve.wait_ge(s("gp"), 1)
            dve.scalar_tensor_tensor(out=g_t1[:, :, :], in0=g_in[:, :, :], scalar=-1.0, in1=g_in[:, :, :],
                                     op0=ALU.mult, op1=ALU.min).then_inc(s("gp"), 1)
            for h in range(NH):
                dve.wait_ge(s("vtr"), h + 1)
                dve.tensor_copy(acc_kv[:, 8 + h, :], ps[:, 2 + h % 2, :]).then_inc(s("vnat_done"), 1)
            dve.wait_ge(s("gp_act"), 4)
            step(dve.scalar_tensor_tensor(out=g_t1[:, :, :], in0=g_in[:, :, :], scalar=0.0, in1=g_t2[:, :, :],
                                          op0=ALU.max, op1=ALU.add))
            dve.scalar_tensor_tensor(out=g_log[:, :, :], in0=g_t1[:, :, :], scalar=-1.0, in1=bc(alog[:, :], NT),
                                     op0=ALU.mult, op1=ALU.mult).then_inc(s("gp"), 1)
            step(dve.tensor_scalar(beta[:, :, :], beta[:, :, :], 1.0, None, ALU.add))
            step(dve.reciprocal(beta[:, :, :], beta[:, :, :]))
            step(dve.tensor_scalar(nbeta[:, :, :], beta[:, :, :], -1.0, None, ALU.mult))
            dve.wait_ge(s("gc_mm"), 1)
            tot = ps[:, 4, 64:128].rearrange("p (t c) -> p t c", t=NT)
            dve.tensor_copy(gcum[:, :, :], ps[:, 4, 0:64].rearrange("p (t c) -> p t c", t=NT)).then_inc(s("gc_ev"), 1)
            dve.wait_ge(s("gc_ev"), 1)
            dve.tensor_tensor(e_tail[:, :, :], tot, gcum[:, :, :], ALU.subtract).then_inc(s("gc_ev"), 1)
            dve.tensor_copy(e_last[:, :, :], tot).then_inc(s("gc_ev"), 1)
            for j in range(12):
                dve.wait_ge(s("l2_rs"), j // 4 + 1)
                if j < 8:
                    dve.tensor_tensor(acc_kv[:, j, :], acc_kv[:, j, :], l2b[:, j, :], ALU.mult
                                      ).then_inc(s("l2_done"), 1)
                else:
                    q2 = acc_x[:, 2 * (j - 8):2 * (j - 8) + 2, :].rearrange("p a c -> p (a c)")
                    dve.scalar_tensor_tensor(out=q2, in0=q2, scalar=float(P) ** -0.5, in1=l2b[:, j, :],
                                             op0=ALU.mult, op1=ALU.mult).then_inc(s("l2_done"), 1)
            dve.wait_ge(s("gp_act"), 7)
            dve.tensor_scalar(neg_eg[:, :, :], neg_eg[:, :, :], -1.0, None, ALU.mult).then_inc(s("gp_sel"), 1)
            q4 = "p (t c) -> p t c"

            def kk_evac(h):
                dve.wait_ge(s("kk_mm"), 2 * h + 1)
                if h:
                    dve.wait_ge(s("am_pool"), 2 * h)
                dve.wait_ge(s("masks"), N_MASKS)
                for d, m in ((0, SU), (1, SL)):
                    dve.tensor_tensor(KK[:, d, :].rearrange(q4, t=4), ps[:, 6, :].rearrange(q4, t=4),
                                      bc(tri[:, m, :], 4), ALU.mult).then_inc(s("kk_ev"), 1)
                dve.wait_ge(s("kk_mm"), 2 * h + 2)
                for d, m in ((0, UI), (1, LI)):
                    dve.tensor_tensor(QK[:, d, :].rearrange(q4, t=2), ps[:, 7, 0:T].rearrange(q4, t=2),
                                      bc(tri[:, m, :], 2), ALU.mult).then_inc(s("kk_ev"), 1)

            def gb_evac(r):
                h, d = r // 2, r % 2
                dve.wait_ge(s("gb_mm"), r + 1)
                if r >= 2:
                    dve.wait_ge(s("t1_mm"), r - 1)
                for t in range(NCH):
                    cs = slice(t * P, (t + 1) * P)
                    dve.tensor_scalar(Eb[:, r % 2, cs], ps[:, gb_bank(r), cs], gcum[:, t, 8 * d + h:8 * d + h + 1],
                                      0.0, ALU.subtract, ALU.min).then_inc(s("gb_ev"), 1)

            def mn_evac(r):
                h, d = r // 2, r % 2
                dve.wait_ge(s("t1_mm"), r + 1)
                if r:
                    dve.wait_ge(s("t2_mm"), r)
                    dve.wait_ge(s("x0"), 2 * r)
                dve.tensor_tensor(Mn[:, :].rearrange(q4, t=4), ps[:, t1_bank(r), :].rearrange(q4, t=4),
                                  bc_in(nbeta[:, :, 8 * d + h], P), ALU.mult).then_inc(s("mn_ev"), 1)

            def start_inverse(r, which):
                d, g2, q = r % 2, (r // 4) % 2, r % 4
                if which == 0:
                    dst, src, m = Xb[:, g2, q, :], Mn[:, :], (m_low, m_up)[d]
                    name = "x0"
                    if r >= 8:
                        dve.wait_ge(s("x_upd"), inverted(r - 8 + 3 - r % 4))
                    dve.wait_ge(s("mn_ev"), r + 1)
                else:
                    dst, src, m = XT[:, r, :], MT[:, g2, q, :], (m_up, m_low)[d]
                    name = "xt0"
                    dve.wait_ge(s("mt_ev"), r + 1)
                dst, src = dst.rearrange(q4, t=4), src.rearrange(q4, t=4)
                dve.tensor_tensor(dst, src, bc(m[:, 0, :], 4), ALU.mult).then_inc(s(name), 1)
                dve.wait_ge(s(name), 2 * r + 1)
                dve.tensor_tensor(dst, dst, bc(ident[:, :], 4), ALU.add).then_inc(s(name), 1)

            def p_evac(G, i):
                no, lv, d = 24 * G + i, 1 + i // 4, i % 2
                dve.wait_ge(s("p_mm"), no + 1)
                if no >= 2:
                    dve.wait_ge(s("y_mm"), no - 1)
                dve.tensor_tensor(Pb[:, no % 2, :].rearrange(q4, t=4), ps[:, no % 2, :].rearrange(q4, t=4),
                                  bc((m_low, m_up)[d][:, lv, :], 4), ALU.mult).then_inc(s("p_ev"), 1)

            def x_update(G, i):
                no, lv, q = 24 * G + i, 1 + i // 4, i % 4
                r = 4 * G + q
                h, d = r // 2, r % 2
                dve.wait_ge(s("y_mm"), no + 1)
                xt = XT[:, r, :]
                if lv < LEVELS:
                    xx = Xb[:, G % 2, q, :]
                    dve.tensor_tensor(xx, xx, ps[:, 2 + no % 2, :], ALU.add)
                    dve.tensor_tensor(xt, xt, ps[:, 4 + no % 2, :], ALU.add).then_inc(s("x_upd"), 1)
                else:
                    step(dve.tensor_tensor(xt, xt, ps[:, 4 + no % 2, :], ALU.add))
                    xt = xt.rearrange(q4, t=4)
                    dve.tensor_tensor(xt, xt, bc_in(beta[:, :, 8 * d + h], P), ALU.mult).then_inc(s("x_upd"), 1)

            dve.wait_ge(s("l2_done"), 12)
            for G in range(-1, 4):
                for i in range(26):
                    if G >= 0:
                        if i < 24:
                            p_evac(G, i)
                        if i >= 2:
                            x_update(G, i - 2)
                    if G < 3:
                        q, j = i // 6, i % 6
                        r = 4 * (G + 1) + q
                        if j == 0 and q:
                            start_inverse(r - 1, 1)
                        if q < 4:
                            if j == 0 and q % 2 == 0:
                                kk_evac(r // 2)
                            if j == 1:
                                gb_evac(r)
                            if j == 4:
                                mn_evac(r)
                            if j == 5:
                                start_inverse(r, 0)
            dve.wait_ge(s("red_mm"), 1)
            dve.tensor_tensor(shift2[:, :], ps[:, 7, 0:KT], col_a[:, 6, :], ALU.add).then_inc(s("red_ev"), 1)
            dve.tensor_tensor(scale2[:, :], ps[:, 7, KT:2 * KT], col_a[:, 7, :], ALU.add).then_inc(s("red_ev"), 1)
            dve.wait_ge(s("red_ev"), 2)
            dve.tensor_tensor(scale2[:, :], scale2[:, :], col_a[:, 3, :], ALU.mult).then_inc(s("red_ev"), 1)
            for n in range(NCHAIN):
                h, d = n // 2, 1 - n % 2
                dve.wait_ge(s("er_exp"), n + 1)
                dst = qd_b[:, h, :] if d else acc_x[:, h, :]
                if d == 0:
                    dve.wait_ge(s("qd"), n)
                else:
                    dve.wait_ge(s("x_upd"), inverted(NCHAIN - 1))
                dve.tensor_tensor(dst, acc_x[:, h, :], eg_row[:, n % 2, :], ALU.mult).then_inc(s("qd"), 1)
            def gate_half(kk):
                n = 2 * kk
                dve.wait_ge(g1_in[n % 4], 16 * (n // 4 + 1))
                if kk == 0:
                    dve.wait_ge(s("g1_b"), 16)
                else:
                    dve.wait_ge(s("ada_dve"), kk)
                dve.scalar_tensor_tensor(out=g1_acc[:, 0:HALF], in0=g1_tile[:, n % 4, :], scalar=cond[:, kk, 0:1],
                                         in1=g1_acc[:, 0:HALF], op0=ALU.mult, op1=ALU.add).then_inc(s("ada_dve"), 1)

            for st in range(4):
                for g in range(4):
                    if st:
                        dve.wait_ge(s("ks_mm"), 4 * (st - 1) + g + 1)
                        for q in range(4):
                            h, d = 2 * g + q // 2, q % 2
                            t = chunk_at(st, d)
                            ins = dve.scalar_tensor_tensor(
                                out=rb[:, g, q * P:(q + 1) * P], in0=ps[:, g, q * P:(q + 1) * P],
                                scalar=neg_eg[:, t, 8 * d + h:8 * d + h + 1], in1=acc_kv[:, 8 + h, t * P:(t + 1) * P],
                                op0=ALU.mult, op1=ALU.add)
                        ins.then_inc(s("r_ev"), 1)
                for g in range(4):
                    dve.wait_ge(s("vn_mm"), 4 * st + g + 1)
                    if st:
                        dve.wait_ge(s("vt_ev"), 4 * (4 * (st - 1) + g + 1))
                    dve.tensor_copy(vn[:, g, :], ps[:, g, :]).then_inc(s("vn_ev"), 1)
                    gate_half(4 * st + g)
                if st == 3:
                    break
                for g in range(4):
                    dve.wait_ge(s("su_mm"), 4 * st + g + 1)
                    if st == 0:
                        dve.tensor_copy(Sb[:, 4 * g:4 * g + 4, :].rearrange("p a b -> p (a b)"), ps[:, g, :]
                                        ).then_inc(s("s_ev"), 1)
                        continue
                    dve.wait_ge(s("s_ev"), 4 * (st - 1) + g + 1)
                    for q in range(4):
                        h, d = 2 * g + q // 2, q % 2
                        t = chunk_at(st, d)
                        ins = dve.scalar_tensor_tensor(
                            out=Sb[:, 4 * g + q, :], in0=Sb[:, 4 * g + q, :],
                            scalar=e_last[:, t, 8 * d + h:8 * d + h + 1], in1=ps[:, g, q * P:(q + 1) * P],
                            op0=ALU.mult, op1=ALU.add)
                    ins.then_inc(s("s_ev"), 1)
            dve.wait_ge(s("o_mm"), 1)
            for i in range(4):
                dve.tensor_copy(o_sb[:, 2 * i:2 * i + 2, :].rearrange("p a b -> p (a b)"), ps[:, 4 + i, :]
                                ).then_inc(s("o_ev"), 1)
            dve.wait_ge(s("o_sqd"), 1)
            dve.wait_ge(s("o_ev"), 4)
            dve.wait_ge(s("zsilu"), 1)
            step(dve.scalar_tensor_tensor(out=o_sb[:, :, :], in0=o_sb[:, :, :], scalar=onorm[:, 0:1],
                                          in1=acc_x[:, 8:16, :], op0=ALU.mult, op1=ALU.mult))
            dve.wait_ge(s("on_rs"), 5)
            dve.tensor_tensor(mixT[:, 0:8, :], o_sb[:, :, :], o_rs[:, :, :], ALU.mult).then_inc(s("mix_lin"), 1)
            for kt in range(KT):
                dve.wait_ge(s("mixh"), kt + 1)
                dve.tensor_tensor(mix_lo[:, kt, :], mixT[:, kt, :], mix_hi[:, kt, :].bitcast(F32), ALU.subtract
                                  ).then_inc(s("mixl"), 1)

            def y_evac(ch, i):
                tk, cc = i // 2, i % 2
                n_y = 4 * ch + i
                cs = slice(ch * 1024 + cc * 512, ch * 1024 + (cc + 1) * 512)
                wait_used(dve, 2 * N_IN + KT * (ch + 1) - 1)
                dve.wait_ge(s("g1_ev"), 4)
                if n_y >= 2:
                    dve.wait_ge(s("x2_done"), n_y - 1)
                step(dve.tensor_tensor(yt[:, n_y % 2, :], ps[:, 4 * ch + i, :], gate1[:, cs], ALU.mult))
                dve.wait_ge(s("xres_in"), 16)
                dve.tensor_tensor(x2[:, tk, cs], x2[:, tk, cs], yt[:, n_y % 2, :], ALU.add).then_inc(s("x2_done"), 1)

            O2 = 2 * N_IN
            for j in range(2 * N_OUT):
                lo_split(dve, O2 + j)
                if KT + 2 <= j < KT + 6:
                    y_evac(0, j - KT - 2)
            for i in range(4):
                y_evac(1, i)
            H0 = 2 * (N_IN + N_OUT)
            E0 = H0 + 2 * N_UP

            def mlp_lo(it, k, h0, per):
                n2 = h0 + k
                hs = slice((n2 % 2) * HALF, (n2 % 2 + 1) * HALF)
                dve.wait_ge(s("hi_done"), it * per + n2 + 1)
                dve.tensor_tensor(w_lo[:, n2 % NHL, :], raw[:, (n2 // 2) % NRAW, hs],
                                  w_hi[:, n2 % NHL, :].bitcast(F32), ALU.subtract).then_inc(s("lo_done"), 1)

            dve.wait_ge(s("rms2"), 1)
            for t in range(2):
                dve.tensor_scalar(xs2[:, t, :], x2[:, t, :], rms[:, t:t + 1], None, ALU.mult).then_inc(s("xs2_done"), 1)
            for kt in range(KT + 2):
                if kt < KT:
                    dve.wait_ge(s("t3_mm"), kt // 2 + 1)
                    dve.tensor_scalar(xT2[:, kt, :], ps[:, 4 + (kt // 2) % 4, (kt % 2) * T:(kt % 2 + 1) * T],
                                      scale2[:, kt:kt + 1], shift2[:, kt:kt + 1], ALU.mult, ALU.add
                                      ).then_inc(s("mod2"), 1)
                if kt >= 2:
                    dve.wait_ge(s("xn2h"), kt - 1)
                    dve.tensor_tensor(xn2_lo[:, kt - 2, :], xT2[:, kt - 2, :], xn2_hi[:, kt - 2, :].bitcast(F32),
                                      ALU.subtract).then_inc(s("xn2l"), 1)
                if kt in (2, 4, 6):
                    mlp_lo(0, kt // 2 - 1, H0, 16)
            def up_dve(it, ahead):
                for k in range(16):
                    if k < ahead:
                        mlp_lo(it, k + 3, H0, 16)
                    if k % 8 == 4:
                        j = k // 8
                        dve.wait_ge(gate_in[j], it * 16 + 16)
                        dve.wait_ge(s("ada_dve"), it * 2 + KT + j)
                        dve.scalar_tensor_tensor(out=g2_acc[:, :], in0=ada[:, j, :],
                                                 scalar=cond[:, ds(it * 2 + j, 1), 0], in1=g2_acc[:, :],
                                                 op0=ALU.mult, op1=ALU.add).then_inc(s("ada_dve"), 1)
                    if k % 8 == 7:
                        for i in range(2):
                            bank = 2 * (k // 8) + i
                            hh = hT[:, ds(it * 8 + 2 * bank, 2), :].rearrange("p a b -> p (a b)")
                            dve.wait_ge(s("relu_a"), it * 4 + bank + 1)
                            dve.tensor_tensor(hh, hh, hh, ALU.mult).then_inc(s("relu_v"), 1)

            dve.wait_ge(s("g2_b"), 16)
            with dve.Fori(0, 7) as it:
                up_dve(it, 16)
            up_dve(7, 13)

            def z_evac(ch):
                wait_used(dve, E0 + 64 * (ch + 1) - 1)
                dve.wait_ge(s("g2_ev"), 4)
                for i in range(4):
                    tk, cc = i // 2, i % 2
                    cs = slice(ch * 1024 + cc * 512, ch * 1024 + (cc + 1) * 512)
                    step(dve.tensor_tensor(yt2[:, i % 2, :], ps[:, 4 * ch + i, :], gate2[:, cs], ALU.mult))
                    dve.tensor_tensor(x2[:, tk, cs], x2[:, tk, cs], yt2[:, i % 2, :], ALU.add).then_inc(s("fin_a"), 1)

            def down_dve(it, ch, k):
                mlp_lo(it, k, E0 + 64 * ch, 8)
                dve.wait_ge(s("hh"), it * 8 + 64 * ch + k + 1)
                dve.tensor_tensor(h_lo[:, k % 4, :], hT[:, ds(it * 8 + k, 1), :].rearrange("p a b -> p (a b)"),
                                  h_hi[:, k % 4, :].bitcast(F32), ALU.subtract).then_inc(s("hl"), 1)

            with dve.Fori(0, 8) as it:
                for k in range(8):
                    down_dve(it, 0, k)
            for k in range(8):
                down_dve(0, 1, k)
                if k == 3:
                    z_evac(0)
            with dve.Fori(1, 8) as it:
                for k in range(8):
                    down_dve(it, 1, k)
            z_evac(1)
            dve.wait_ge(s("fin_in"), 16)
            dve.wait_ge(s("rms2"), 2)
            for t in range(2):
                dve.scalar_tensor_tensor(out=x2[:, t, :], in0=x2[:, t, :], scalar=rms[:, 2 + t:3 + t],
                                         in1=fin_w[:, :], op0=ALU.mult, op1=ALU.mult).then_inc(s("fin_c"), 1)

        @block.tensor
        def _(pe):
            mm = pe.matmul

            def three(o, xh, xl, wh, wl, start, stop, x_stationary):
                pairs = ((xh, wh), (xh, wl), (xl, wh)) if x_stationary else ((wh, xh), (wh, xl), (wl, xh))
                for i, (l, r) in enumerate(pairs):
                    ins = mm(o, l, r, start=start and i == 0, stop=stop and i == 2, skip_group_check=True)
                return ins

            pe.wait_ge(s("const_done"), 1)
            pe.wait_ge(s("rows_in"), 160)
            pe.transpose(ps[:, 6, 0:P], rows_a[:, :], ident[:, :])
            pe.transpose(ps[:, 6, P:2 * P], rows_b[:, :], ident[:, :]).then_inc(s("rowsT"), 1)
            def inputs_turned():
                pe.wait_ge(s("xs_done"), NT)
                for kt in range(KT):
                    if kt >= 4:
                        pe.wait_ge(s("xt_dve" if kt % 2 else "xt_act"), (kt - 4) // 2 + 1)
                    for t in range(NT):
                        ins = pe.transpose(ps[:, kt % 4, t * P:(t + 1) * P], x_nat[:, t, kt * P:(kt + 1) * P],
                                           ident[:, :])
                    ins.then_inc(s("xt_mm"), 1)
                    if kt % 4 == 3:
                        ada_mod(3 + kt // 4)

            def ada_mod(j):
                pe.wait_ge(mod0_in[j], 16)
                part, g = j // 4, j % 4
                for kk in range(4):
                    for ct in range(4):
                        o = ps[:, 4, 8 * part + 2 * ct:8 * part + 2 * ct + 2]
                        c0 = kk * 512 + ct * P
                        ins = mm(o, mod0[:, j, c0:c0 + P], cond[:, 4 * g + kk, :],
                                 start=(j == 0 and kk == 0 and ct == 0), stop=(g == 3 and kk == 3),
                                 skip_group_check=True)
                ins.then_inc(s("ada_pe"), 1)

            def reduce_mod(b):
                pe.wait_ge(s("mod_half"), 2 * 16 * b)
                pe.wait_ge(s("modc_done"), b)
                for part in range(2):
                    for ct in range(4):
                        for j in range(2):
                            c0 = 8 * part + 2 * ct + j
                            ins = mm(ps[:, 4, c0:c0 + 1], mod_acc[:, 2 * part + j, ct * P:(ct + 1) * P], ones[:, 0:1],
                                     start=True, stop=True)
                ins.then_inc(s("ada_pe"), 1)

            pe.wait_ge(s("cond_done"), 1)
            for j in range(3):
                ada_mod(j)
            inputs_turned()
            ada_mod(7)

            def in_half(b, m):
                n2 = HB * b + m
                both = IN_UNITS[unit_of(n2)][1]
                wh = w_hi[:, n2 % NHL, :].rearrange("p (k c) -> p k c", k=4)
                wl = w_lo[:, n2 % NHL, :].rearrange("p (k c) -> p k c", k=4)
                nn = 2 * T if both else T
                wait_lo(pe, n2)
                for ct in range(2):
                    no = PLAN[n2][ct if both else 0]
                    if no >= 4 and (both or ct == 0):
                        if no - 4 < N0:
                            pe.wait_ge(s("pj_act"), no - 4 + 1)
                        else:
                            pe.wait_ge(s("pj_dve"), no - 4 - N0 + 1)
                    o = ps[:, no % 4, :] if both else ps[:, no % 4, ct * T:(ct + 1) * T]
                    cs = slice(ct * P, (ct + 1) * P)
                    for k in range(BK):
                        ins = three(o, xn_hi[:, k, 0:nn], xn_lo[:, k, 0:nn], wh[:, k, cs], wl[:, k, cs],
                                    k == 0 and (both or ct == 0), k == BK - 1, False)
                    if both and ct == 0:
                        ins.then_inc(s("pj"), 1)
                return ins

            for b in range(NB):
                if b == 0:
                    pe.wait_ge(s("wab_l"), 1)
                    pe.wait_ge(s("xt_act"), KT // 2)
                    pe.wait_ge(s("xt_dve"), KT // 2)
                for k in range(BK):
                    pe.wait_ge(s("xnl"), BK * b + k + 1)
                    for t in range(NT):
                        ts = slice(t * P, (t + 1) * P)
                        ins = three(ps[:, 5, t * 32:(t + 1) * 32], xn_hi[:, k, ts], xn_lo[:, k, ts],
                                    wab_hi[:, BK * b + k, :], wab_lo[:, BK * b + k, :],
                                    b == 0 and k == 0 and t == 0, b == NB - 1 and k == BK - 1, True)
                if b == NB - 1:
                    ins.then_inc(s("ab_done"), 1)
                for m in range(HB):
                    in_half(b, m).then_inc(s("pj"), 1)
                    if b < NB - 1 and m == 16:
                        reduce_mod(b + 1)
            pe.wait_ge(s("xt_act"), KT // 2)
            for h in range(NH):
                pe.wait_ge(s("silu"), 8 + h + 1)
                pe.wait_ge(s("pj_dve"), PJ_DVE)
                if h >= 2:
                    pe.wait_ge(s("vnat_done"), h - 1)
                for t in range(NCH):
                    ts = slice(t * P, (t + 1) * P)
                    ins = pe.transpose(ps[:, 2 + h % 2, ts], acc_kv[:, 8 + h, ts], ident[:, :])
                ins.then_inc(s("vtr"), 1)
            pe.wait_ge(s("masks"), N_MASKS)
            pe.wait_ge(s("gp"), 4)
            gc = ps[:, 4, 0:64].rearrange("p (t c) -> p t c", t=NT)
            mm(gc[:, :, 0:8], tri[:, UI, :], g_log[:, :, 0:8], start=True, stop=True)
            mm(gc[:, :, 8:16], tri[:, LI, :], g_log[:, :, 8:16], start=True, stop=True)
            mm(ps[:, 4, 64:128], ones[:, :], g_log[:, :, :].rearrange("p t c -> p (t c)"), start=True, stop=True
               ).then_inc(s("gc_mm"), 1)
            pe.wait_ge(s("gc_ev"), 1)
            for t in range(NT):
                ins = pe.transpose(ps[0:16, 5, t * P:(t + 1) * P], gcum[:, t, :], ident[:, :])
            ins.then_inc(s("gcT_mm"), 1)
            for j in range(12):
                pe.wait_ge(s("l2_sq"), j + 1)
                if j >= 2:
                    pe.wait_ge(s("l2_ln"), j - 1)
                mm(ps[:, j % 2, :], ones[:, :], l2b[:, j, :], start=True, stop=True).then_inc(s("l2_mm"), 1)
            pe.wait_ge(s("l2_done"), 12)
            pe.wait_ge(s("gcT_ev"), 1)
            pe.wait_ge(s("vnat_done"), NH)

            def cs(t):
                return slice(t * P, (t + 1) * P)

            def kk_products(h):
                if h:
                    pe.wait_ge(s("mn_ev"), 2 * h)
                for t in range(NCH):
                    k = acc_kv[:, h, cs(t)]
                    ins = mm(ps[:, 6, cs(t)], k, k, start=True, stop=True)
                ins.then_inc(s("kk_mm"), 1)
                if h:
                    pe.wait_ge(s("mt_ev"), 2 * h)
                for t in range(2):
                    ins = mm(ps[:, 7, cs(t)], acc_kv[:, h, cs(t)], acc_x[:, h, cs(t)], start=True, stop=True)
                ins.then_inc(s("kk_mm"), 1)

            def decay_rows(r):
                h, d = r // 2, r % 2
                if d == 0:
                    pe.wait_ge(s("kk_ev"), 4 * h + 2)
                else:
                    pe.wait_ge(s("mn_ev"), r)
                mm(ps[:, gb_bank(r), :], sel[:, 8 * d + h, :], gcT[:, :], start=True, stop=True
                   ).then_inc(s("gb_mm"), 1)

            def turn1(r):
                pe.wait_ge(s("am_pool"), r + 1)
                if r % 2 == 0:
                    pe.wait_ge(s("kk_ev"), 4 * (r // 2) + 4)
                else:
                    pe.wait_ge(s("mt_ev"), r)
                for t in range(NCH):
                    ins = pe.transpose(ps[:, t1_bank(r), cs(t)], Eb[:, r % 2, cs(t)], ident[:, :])
                ins.then_inc(s("t1_mm"), 1)

            def turn2(r):
                pe.wait_ge(s("mn_ev"), r + 1)
                pe.wait_ge(s("gb_ev"), 4 * (r + 1))
                for t in range(NCH):
                    ins = pe.transpose(ps[:, t2_bank(r), cs(t)], Mn[:, cs(t)], ident[:, :])
                ins.then_inc(s("t2_mm"), 1)

            def p_products(G, i):
                no, q = 24 * G + i, i % 4
                if i < 4:
                    pe.wait_ge(s("x0"), 2 * (4 * G + q + 1))
                    pe.wait_ge(s("xt0"), 2 * (4 * G + q + 1))
                else:
                    pe.wait_ge(s("x_upd"), no - 4 + 1)
                if no >= 2:
                    pe.wait_ge(s("p_ev"), no - 1)
                for t in range(NCH):
                    ins = mm(ps[:, no % 2, cs(t)], MT[:, G % 2, q, cs(t)], Xb[:, G % 2, q, cs(t)], start=True, stop=True)
                ins.then_inc(s("p_mm"), 1)

            def y_products(G, i):
                no, q, lv = 24 * G + i, i % 4, 1 + i // 4
                pe.wait_ge(s("p_ev"), no + 1)
                if no >= 2:
                    pe.wait_ge(s("x_upd"), no - 1)
                for t in range(NCH):
                    if lv < LEVELS:
                        mm(ps[:, 2 + no % 2, cs(t)], XT[:, 4 * G + q, cs(t)], Pb[:, no % 2, cs(t)], start=True, stop=True)
                for t in range(NCH):
                    ins = mm(ps[:, 4 + no % 2, cs(t)], Pb[:, no % 2, cs(t)], XT[:, 4 * G + q, cs(t)], start=True, stop=True)
                ins.then_inc(s("y_mm"), 1)

            for G in range(-1, 4):
                for i in range(26):
                    if G >= 0:
                        if i < 24:
                            p_products(G, i)
                        if i >= 2:
                            y_products(G, i - 2)
                    if G < 3:
                        q, j = i // 6, i % 6
                        r = 4 * (G + 1) + q
                        if q < 4:
                            if j == 0 and q % 2 == 0:
                                kk_products(r // 2)
                            if j == 1:
                                decay_rows(r)
                            if j == 4:
                                turn1(r)
                            if j == 5:
                                turn2(r)
            pe.wait_ge(s("row_sum"), 64)
            pe.wait_ge(s("mt_ev"), NCHAIN)
            pe.wait_ge(s("mn_ev"), NCHAIN)
            for i in range(2 * KT):
                ins = mm(ps[:, 7, i:i + 1], row_acc[:, i // KT, (i % KT) * P:(i % KT + 1) * P], ones[:, 0:1],
                         start=True, stop=True)
            ins.then_inc(s("red_mm"), 1)
            pe.wait_ge(s("x_upd"), inverted(NCHAIN - 1))
            for n in range(NCHAIN):
                h, d = n // 2, 1 - n % 2
                if n >= 2:
                    pe.wait_ge(s("er_exp"), n - 1)
                mm(ps[:, n % 2, 0:T], sel[:, 8 * d + h, :], gcT[:, 0:T], start=True, stop=True).then_inc(s("er_mm"), 1)
                if n < NH:
                    if n >= 2:
                        pe.wait_ge(s("kn_ev"), n - 1)
                    for t in range(NCH):
                        ins = pe.transpose(ps[:, 2 + n % 2, cs(t)], acc_kv[:, n, cs(t)], ident[:, :])
                    ins.then_inc(s("ktr"), 1)
            pe.wait_ge(s("kn_ev"), NH)
            pe.wait_ge(s("er_exp"), NCHAIN)
            pe.wait_ge(s("qd"), NCHAIN)
            pe.wait_ge(s("red_ev"), 2)
            for st in range(4):
                for g in range(4):
                    if st:
                        pe.wait_ge(s("s_ev"), 4 * (st - 1) + g + 1)
                        for q in range(4):
                            h, d = 2 * g + q // 2, q % 2
                            ins = mm(ps[:, g, cs(q)], acc_kv[:, h, cs(chunk_at(st, d))], Sb[:, 4 * g + q, :],
                                     start=True, stop=True)
                        ins.then_inc(s("ks_mm"), 1)
                for g in range(4):
                    if st:
                        pe.wait_ge(s("r_ev"), 4 * (st - 1) + g + 1)
                    for q in range(4):
                        h, d = 2 * g + q // 2, q % 2
                        t = chunk_at(st, d)
                        rhs = rb[:, g, cs(q)] if st else acc_kv[:, 8 + h, cs(t)]
                        ins = mm(ps[:, g, cs(q)], XT[:, 4 * g + q, cs(t)], rhs, start=True, stop=True)
                    ins.then_inc(s("vn_mm"), 1)
                for g in range(4):
                    pe.wait_ge(s("vn_ev"), 4 * st + g + 1)
                    if st >= 2:
                        for q in range(4):
                            h, d = 2 * g + q // 2, q % 2
                            t = chunk_at(st, d)
                            o = ps[:, 4 + g, (q // 2) * T + t * P:(q // 2) * T + (t + 1) * P]
                            qd = qd_b[:, h, cs(t)] if d else acc_x[:, h, cs(t)]
                            mm(o, Sb[:, 4 * g + q, :], qd, start=(st == 2 and q == 0), stop=False, skip_group_check=True)
                            ins = mm(o, vn[:, g, cs(q)], At[:, 4 * g + q, cs(t)], start=False, stop=(st == 3),
                                     skip_group_check=True)
                    if st < 3:
                        pe.wait_ge(s("vt_ev"), 4 * (4 * st + g + 1))
                        for q in range(4):
                            h, d = 2 * g + q // 2, q % 2
                            ins = mm(ps[:, g, cs(q)], k_nat[:, h, chunk_at(st, d), :], vt[:, g, cs(q)],
                                     start=True, stop=True)
                        ins.then_inc(s("su_mm"), 1)
            ins.then_inc(s("o_mm"), 1)
            pe.wait_ge(s("ada_dve"), KT)
            pe.wait_ge(s("g1_pool"), KT)
            for i in range(4):
                if i >= 2:
                    pe.wait_ge(s("g1_ev"), i - 1)
                mm(ps[:, 2 + i % 2, :], ones[:, :], g1_acc[:, i * 512:(i + 1) * 512], start=True, stop=True
                   ).then_inc(s("g1_mm"), 1)

            pe.wait_ge(s("o_sqd"), 1)
            for i in range(4):
                mm(ps[:, 4 + i, :], ones[:, :], o_sq[:, 2 * i:2 * i + 2, :].rearrange("p a b -> p (a b)"),
                   start=True, stop=True).then_inc(s("on_mm"), 1)
            pe.wait_ge(s("pool_w_in"), 16)
            for i in range(8):
                g, o_ = i // 2, i % 2
                pe.wait_ge(s("pool_d"), g + 1)
                if i >= 2:
                    pe.wait_ge(s("mix_pool"), i - 1)
                for it in range(2):
                    c0 = (2 * g + it) * 256 + o_ * P
                    ins = mm(ps[:, i % 2, 0:T], ada[:, 1, c0:c0 + P], acc_x[:, 16 + 2 * g + it, :],
                             start=(it == 0), stop=(it == 1))
                ins.then_inc(s("pw_mm"), 1)

            def wide_half(slot, xh, xl, bank0, start, stop):
                for tk in range(2):
                    for cc in range(2):
                        ws = slice(cc * 512, (cc + 1) * 512)
                        ts = slice(tk * P, (tk + 1) * P)
                        ins = three(ps[:, bank0 + 2 * tk + cc, :], xh[:, ts], xl[:, ts], w_hi[:, slot, ws],
                                    w_lo[:, slot, ws], start, stop, True)
                return ins

            pe.wait_ge(s("mix_pool"), 8)
            pe.wait_ge(s("on_rs"), 4)
            pe.wait_ge(s("g1_ev"), 4)
            for ch in range(2):
                for kt in range(KT):
                    n2 = 2 * N_IN + KT * ch + kt
                    pe.wait_ge(s("mixl"), kt + 1)
                    wait_lo(pe, n2)
                    wide_half(n2 % NHL, mix_hi[:, kt, :], mix_lo[:, kt, :], 4 * ch, kt == 0, kt == KT - 1
                              ).then_inc(s("w_used"), 1)
            pe.wait_ge(s("xs2_done"), 2)
            for i in range(8):
                if i >= 4:
                    pe.wait_ge(s("mod2"), 2 * (i - 4) + 2)
                for j in range(4):
                    kt, t = 2 * i + j // 2, j % 2
                    ins = pe.transpose(ps[:, 4 + i % 4, j * P:(j + 1) * P], xs2[:, t, kt * P:(kt + 1) * P], ident[:, :])
                ins.then_inc(s("t3_mm"), 1)
            H0 = 2 * (N_IN + N_OUT)
            E0 = H0 + 2 * N_UP

            def up_pe(it, first):
                for k in range(16):
                    cc, m = k // 8, k % 8
                    pe.wait_ge(s("lo_done"), it * 16 + LO + H0 + k + 1)
                    if first and cc == 0:
                        pe.wait_ge(s("xn2l"), 2 * m + 2)
                    if m == 0 and not first:
                        pe.wait_ge(s("relu_a"), it * 4 + 2 * cc + 2 - 4)
                    slot = (H0 + k) % NHL
                    for j in range(4):
                        o = ps[:, 2 * cc + j // 2, (j % 2) * T:(j % 2 + 1) * T]
                        for kk in range(2):
                            kt, ws = 2 * m + kk, slice(kk * 512 + j * P, kk * 512 + (j + 1) * P)
                            ins = three(o, xn2_hi[:, kt, :], xn2_lo[:, kt, :], w_hi[:, slot, ws], w_lo[:, slot, ws],
                                        m == 0 and kk == 0 and j % 2 == 0, m == 7 and kk == 1, False)
                    ins.then_inc(s("w_used"), 1)

            up_pe(0, True)
            with pe.Fori(1, 8) as it:
                up_pe(it, False)
            pe.wait_ge(s("relu_a"), 32)
            pe.wait_ge(s("zr"), 1)
            pe.wait_ge(s("ada_dve"), 2 * KT)
            pe.wait_ge(s("x2_done"), 8)
            for i in range(4):
                mm(ps[:, 4 + i, :], ones[:, :], g2_acc[:, i * 512:(i + 1) * 512], start=True, stop=True
                   ).then_inc(s("g2_mm"), 1)
            for ch in range(2):
                if ch:
                    pe.wait_ge(s("g2_ev"), 4)
                for i in range(4):
                    mm(ps[:, 4 * ch + i, :], zero_r[:, 0:P], zero_r[:, :], start=True, stop=False, skip_group_check=True)
                with pe.Fori(0, 8) as it:
                    for k in range(8):
                        pe.wait_ge(s("lo_done"), it * 8 + LO + E0 + 64 * ch + k + 1)
                        pe.wait_ge(s("hl"), it * 8 + 64 * ch + k + 1)
                        wide_half((E0 + k) % NHL, h_hi[:, k % 4, :], h_lo[:, k % 4, :], 4 * ch, False, False
                                  ).then_inc(s("w_used"), 1)


_INS = ['x', 'c', 'ctx', 'c_ctx', 'w_ada', 'b_ada', 'norm1_w', 'norm2_w', 'w_in', 'conv_w', 'a_log', 'dt_bias',
        'onorm_w', 'pool_w', 'pool_scale', 'w_out', 'w_up', 'w_down', 'final_norm_w']
_OUTS = [((1, T, D), 'float32')]


def kernel(**inputs):
    import numpy as _np
    import concourse.bacc as _bacc
    from concourse import mybir as _mybir
    from concourse.bass_utils import run_bass_kernel_spmd as _run

    nc = _bacc.Bacc("TRN2", target_bir_lowering=False, num_devices=1)
    arrays, args = {}, []
    for name in _INS:
        a = _np.ascontiguousarray(inputs[name])
        arrays[f"in_{name}_dram"] = a
        args.append(nc.dram_tensor(f"in_{name}_dram", a.shape, _mybir.dt.from_np(a.dtype), kind="ExternalInput").ap())
    for i, (shape, dtype) in enumerate(_OUTS):
        dt = _mybir.dt.from_np(_np.dtype(dtype))
        args.append(nc.dram_tensor(f"out_{i}_dram", shape, dt, kind="ExternalOutput").ap())
    build(nc, *args)
    r = _run(nc, [arrays], core_ids=[0])
    return r.results[0]["out_0_dram"]
```
